# Optimizing a Trainium2 kernel written in Bass

```python
import jax, jax.numpy as jnp
from jax import lax
import numpy as np

D_MODEL = 1024
BATCH = 1
SEQ = 256
DEPTH = 2

CHUNK = 64
MEM_LEN = 256
D_MIX = D_MODEL
D_POOL = D_MIX // 4
D_SCONV = (D_MIX - D_POOL) // 2
D_CONF = D_MIX - D_POOL - D_SCONV
POOL_WINDOWS = (2, 4, 8, 16)
N_POOL_GROUPS = len(POOL_WINDOWS)
POOL_GROUP = D_POOL // N_POOL_GROUPS
SCONV_WIDTH = 3
CONF_WIDTH = 31
SPLITS = (D_POOL, D_POOL + D_SCONV, D_POOL + 2 * D_SCONV, D_POOL + 3 * D_SCONV,
          D_POOL + 3 * D_SCONV + D_CONF)
D_IN = D_POOL + 3 * D_SCONV + 2 * D_CONF
N_MEM_HEADS = 4
MEM_HEAD_DIM = D_MODEL // N_MEM_HEADS
D_FF = 2816
N_EXPERTS = 8
TOP_K = 2
D_FF_EXPERT = 3584
N_DENSE = (DEPTH + 1) // 2
N_MOE = DEPTH // 2
EPS = 1e-6

kernel_name = "hybrid_pool_sconv_conformer_moe_trunk"

def rms_norm(x, g):
    xf = x.astype(jnp.float32)
    y = xf * lax.rsqrt(jnp.mean(xf * xf, axis=-1, keepdims=True) + EPS)
    return (y * g.astype(jnp.float32)).astype(x.dtype)

def layer_norm(x, g, b):
    xf = x.astype(jnp.float32)
    mu = jnp.mean(xf, axis=-1, keepdims=True)
    xc = xf - mu
    y = xc * lax.rsqrt(jnp.mean(xc * xc, axis=-1, keepdims=True) + EPS)
    return (y * g.astype(jnp.float32) + b.astype(jnp.float32)).astype(x.dtype)

def causal_depthwise_conv(x, w):
    k, c = w.shape
    return lax.conv_general_dilated(
        x, w[:, None, :].astype(x.dtype), window_strides=(1,), padding=[(k - 1, 0)],
        dimension_numbers=('NWC', 'WIO', 'NWC'), feature_group_count=c)

def multiscale_pool(u, pool_w, pool_scale):
    b, s, _ = u.shape
    uf = u.astype(jnp.float32).reshape(b, s, N_POOL_GROUPS, POOL_GROUP)
    csum = jnp.cumsum(uf, axis=1)
    t = jnp.arange(s, dtype=jnp.int32)
    means = []
    for g, win in enumerate(POOL_WINDOWS):
        cg = csum[:, :, g]
        lagged = jnp.pad(cg, ((0, 0), (win, 0), (0, 0)))[:, :s]
        count = jnp.minimum(t + 1, win).astype(jnp.float32)[None, :, None]
        means.append((cg - lagged) / count)
    pooled = jnp.stack(means, axis=2) - uf
    y = jnp.einsum('bsgc,gcd->bsgd', pooled, pool_w.astype(jnp.float32)).reshape(b, s, D_POOL)
    return (y * pool_scale.astype(jnp.float32)).astype(u.dtype)

def mixer_block(h, w_in, pool_w, pool_scale, sconv_w, conf_w, conf_b, conf_ln_g, conf_ln_b,
                group_norm_g, w_out):
    z = h @ w_in
    u_pool, u_s, gate_b, gate_c, conf_a, conf_gate = jnp.split(z, SPLITS, axis=-1)
    y_a = multiscale_pool(u_pool, pool_w, pool_scale)
    y_b = gate_b * causal_depthwise_conv(gate_c * u_s, sconv_w)
    hc = conf_a * jax.nn.sigmoid(conf_gate)
    hc = causal_depthwise_conv(hc, conf_w) + conf_b
    y_c = jax.nn.silu(layer_norm(hc, conf_ln_g, conf_ln_b))
    y = jnp.concatenate([
        rms_norm(y_a, group_norm_g[:D_POOL]),
        rms_norm(y_b, group_norm_g[D_POOL:D_POOL + D_SCONV]),
        rms_norm(y_c, group_norm_g[D_POOL + D_SCONV:]),
    ], axis=-1)
    return y @ w_out

def memory_cross_attention(h, mem_k, mem_v, w_q, w_o):
    b, s, _ = h.shape
    q = (h @ w_q).reshape(b, s, N_MEM_HEADS, MEM_HEAD_DIM)
    scores = jnp.einsum('bshd,bmhd->bhsm', q, mem_k).astype(jnp.float32) * (MEM_HEAD_DIM ** -0.5)
    probs = jax.nn.softmax(scores, axis=-1).astype(h.dtype)
    o = jnp.einsum('bhsm,bmhd->bshd', probs, mem_v).reshape(b, s, D_MODEL)
    return o @ w_o

def swiglu(h, w_gu, w_down):
    g, u = jnp.split(h @ w_gu, 2, axis=-1)
    return (jax.nn.silu(g) * u) @ w_down

def moe_swiglu(h, w_router, w_gu, w_down):
    b, s, d = h.shape
    t = h.reshape(b * s, d)
    logits = (t @ w_router).astype(jnp.float32)
    top_vals, top_idx = lax.top_k(logits, TOP_K)
    top_w = jax.nn.softmax(top_vals, axis=-1)
    gates = jnp.sum(jax.nn.one_hot(top_idx, N_EXPERTS, dtype=jnp.float32) * top_w[..., None], axis=1)
    gates = gates.astype(t.dtype)
    out = jnp.zeros_like(t)
    for e in range(N_EXPERTS):
        out = out + gates[:, e:e + 1] * swiglu(t, w_gu[e], w_down[e])
    return out.reshape(b, s, d)

def setup_inputs(seed: int = 0) -> dict:
    key = jax.random.key(seed)
    ks = jax.random.split(key, 32)

    def nrm(k, shape, scale):
        return jax.random.normal(k, shape, dtype=jnp.float32) * scale

    def gain(k, shape):
        return 1.0 + 0.1 * jax.random.normal(k, shape, dtype=jnp.float32)

    L = DEPTH
    return {
        'x': nrm(ks[0], (BATCH, SEQ, D_MODEL), 1.0),
        'mem': nrm(ks[1], (BATCH, MEM_LEN, D_MODEL), 1.0),
        'mix_norm_g': gain(ks[2], (L, D_MODEL)),
        'w_in': nrm(ks[3], (L, D_MODEL, D_IN), D_MODEL ** -0.5),
        'pool_w': nrm(ks[4], (L, N_POOL_GROUPS, POOL_GROUP, POOL_GROUP), POOL_GROUP ** -0.5),
        'pool_scale': gain(ks[5], (L, D_POOL)),
        'sconv_w': nrm(ks[6], (L, SCONV_WIDTH, D_SCONV), SCONV_WIDTH ** -0.5),
        'conf_w': nrm(ks[7], (L, CONF_WIDTH, D_CONF), CONF_WIDTH ** -0.5),
        'conf_b': nrm(ks[8], (L, D_CONF), 0.02),
        'conf_ln_g': gain(ks[9], (L, D_CONF)),
        'conf_ln_b': nrm(ks[10], (L, D_CONF), 0.02),
        'group_norm_g': gain(ks[11], (L, D_MIX)),
        'w_out': nrm(ks[12], (L, D_MIX, D_MODEL), D_MIX ** -0.5),
        'mem_norm_g': gain(ks[13], (D_MODEL,)),
        'w_mem_kv': nrm(ks[14], (D_MODEL, 2 * D_MODEL), D_MODEL ** -0.5),
        'xattn_norm_g': gain(ks[15], (L, D_MODEL)),
        'w_q': nrm(ks[16], (L, D_MODEL, D_MODEL), D_MODEL ** -0.5),
        'w_o': nrm(ks[17], (L, D_MODEL, D_MODEL), D_MODEL ** -0.5),
        'ffn_norm_g': gain(ks[18], (L, D_MODEL)),
        'w_gu_dense': nrm(ks[19], (N_DENSE, D_MODEL, 2 * D_FF), D_MODEL ** -0.5),
        'w_down_dense': nrm(ks[20], (N_DENSE, D_FF, D_MODEL), D_FF ** -0.5),
        'w_router': nrm(ks[21], (N_MOE, D_MODEL, N_EXPERTS), D_MODEL ** -0.5),
        'w_gu_moe': nrm(ks[22], (N_MOE, N_EXPERTS, D_MODEL, 2 * D_FF_EXPERT), D_MODEL ** -0.5),
        'w_down_moe': nrm(ks[23], (N_MOE, N_EXPERTS, D_FF_EXPERT, D_MODEL), D_FF_EXPERT ** -0.5),
        'final_norm_g': gain(ks[24], (D_MODEL,)),
    }

def reference(x, mem, mix_norm_g, w_in, pool_w, pool_scale, sconv_w, conf_w, conf_b, conf_ln_g,
              conf_ln_b, group_norm_g, w_out, mem_norm_g, w_mem_kv, xattn_norm_g, w_q, w_o,
              ffn_norm_g, w_gu_dense, w_down_dense, w_router, w_gu_moe, w_down_moe, final_norm_g):
    b, m, _ = mem.shape
    mem_k, mem_v = jnp.split(rms_norm(mem, mem_norm_g) @ w_mem_kv, 2, axis=-1)
    mem_k = mem_k.reshape(b, m, N_MEM_HEADS, MEM_HEAD_DIM)
    mem_v = mem_v.reshape(b, m, N_MEM_HEADS, MEM_HEAD_DIM)
    for l in range(DEPTH):
        x = x + mixer_block(rms_norm(x, mix_norm_g[l]), w_in[l], pool_w[l], pool_scale[l], sconv_w[l],
                            conf_w[l], conf_b[l], conf_ln_g[l], conf_ln_b[l], group_norm_g[l], w_out[l])
        x = x + memory_cross_attention(rms_norm(x, xattn_norm_g[l]), mem_k, mem_v, w_q[l], w_o[l])
        h = rms_norm(x, ffn_norm_g[l])
        if l % 2 == 0:
            x = x + swiglu(h, w_gu_dense[l // 2], w_down_dense[l // 2])
        else:
            x = x + moe_swiglu(h, w_router[l // 2], w_gu_moe[l // 2], w_down_moe[l // 2])
    return rms_norm(x, final_norm_g)


_drawn_inputs = setup_inputs


def setup_inputs(seed=0):
    import zlib

    import numpy as np

    out = dict(_drawn_inputs(seed))
    spreads = {}
    factors = {'xattn_norm_g': 2.779}
    for name, (base, spread) in spreads.items():
        noise = np.random.default_rng([zlib.crc32(name.encode()), seed]).standard_normal(out[name].shape)
        drawn = base * np.exp(spread * noise) if base else spread * noise
        out[name] = __import__('jax').numpy.asarray(drawn.astype(out[name].dtype))
    for name, factor in factors.items():
        out[name] = (out[name] * factor).astype(out[name].dtype)
    return out
```

```python
from contextlib import ExitStack

import concourse.bass as bass
from concourse import mybir

ALU = mybir.AluOpType
ACT = mybir.ActivationFunctionType
AX = mybir.AxisListType
F32 = mybir.dt.float32
F32R = mybir.dt.float32r
I32 = mybir.dt.int32
U32 = mybir.dt.uint32

P = 128
D = 1024
S = 256
NT = S // P
KD = D // P
EPS = 1e-6
NPOOL, NSC, NCONF = 2, 3, 3
NZ = NPOOL + 3 * NSC + 2 * NCONF
TAPS, SCTAPS = 31, 3
WINDOWS = (2, 4, 8, 16)
HEADS = 4
FF = 2816
NF = FF // 256
E = 8
FE = 3584
CE = FE // 512
SLOTS = 128

PIECE = 2048
RAW = 7
SPLIT = 3
AHEAD = SPLIT - 1

C_ID, C_ONE, C_TRI, C_IOTA, C_INV = 0, 128, 256, 384, 512
C_IOTA8 = C_INV + 2 * S
C_ALL = C_IOTA8 + 8

ROWS = {}
_at = 0
for _name, _n in (("pool_scale", 2 * NPOOL), ("sconv_w", 2 * SCTAPS * NSC), ("conf_b", 2 * NCONF),
                  ("conf_ln_g", 2 * NCONF), ("conf_ln_b", 2 * NCONF), ("group_norm_g", 2 * KD)):
    ROWS[_name] = _at
    _at += _n
NROW = _at
NCW = TAPS * NCONF

WIN_CHUNKS = ((13, 4), (9, 4), (5, 4), (1, 4), (0, 1))
N_WIN, N_KV, N_SQ, N_FFN = 9, 8, 4, 3 * NF


def layer_base(layer):
    q = n = 0
    out = {}
    for m in range(layer + 1):
        for name, pieces, chunks in (("win", N_WIN, len(WIN_CHUNKS)), ("kv", N_KV * (m == 0), 4 * (m == 0)),
                                     ("wout", N_SQ, 2), ("wq", N_SQ, 2), ("wo", N_SQ, 2),
                                     ("ffn", N_FFN * (m == 0), 0)):
            if m == layer:
                out[name] = (q, n)
            q += pieces
            n += chunks
    out["end"] = (q, n)
    return out


BASE = (layer_base(0), layer_base(1))
MOE0 = BASE[1]["end"][0]
NE_PIECE = 6 * CE

MIX_DVE = ("prod", "conv", "sconv_y", "centred", "scaled", "pool_y", "y_pool", "y_sconv", "y_conf",
           "lo_pool", "lo_sconv", "lo_conf")
MIX_ACT = ("mean", "conf_sq", "conf_sd", "silu", "pool_sq", "pool_sd", "sconv_sq", "sconv_sd",
           "rms_sq", "rms_sd", "hi_pool", "hi_sconv", "hi_conf")
MIX_PE = ("mean", "var", "pool", "pool_ssq", "sconv_ssq", "rms_ssq")


def step(steps, name, layer):
    return layer * len(steps) + steps.index(name) + 1


def ffn_piece(kind, j):
    if kind == "down":
        return 3 * (j + 1) + 1 if j < NF - 1 else 3 * NF - 1
    return (0 if j == 0 else 3 * j - 1) + (kind == "up")


def trunk(nc, x, mem, mix_norm_g, w_in, pool_w, pool_scale, sconv_w, conf_w, conf_b, conf_ln_g,
          conf_ln_b, group_norm_g, w_out, mem_norm_g, w_mem_kv, xattn_norm_g, w_q, w_o, ffn_norm_g,
          w_gu_dense, w_down_dense, w_router, w_gu_moe, w_down_moe, final_norm_g, table, out):
    with ExitStack() as ctx:
        def sb(name, shape, dt=F32, scope=ctx):
            return scope.enter_context(nc.sbuf_tensor(name, shape, dt))

        def sem(name):
            return ctx.enter_context(nc.semaphore(name))

        raw = [sb(f"raw{i}", [P, PIECE]) for i in range(RAW)]
        w_hi = [sb(f"w_hi{i}", [P, PIECE], F32R) for i in range(SPLIT)]
        w_lo = [sb(f"w_lo{i}", [P, PIECE], F32R) for i in range(SPLIT)]
        res = sb("res", [P, NT, D])
        xn = sb("xn", [P, NT, D])
        gain = sb("gain", [P, D])
        act_hi = sb("act_hi", [P, KD, S], F32R)
        act_lo = sb("act_lo", [P, KD, S], F32R)
        cst = sb("cst", [P, C_ALL])
        rows = sb("rows", [P, 3, P])
        par = sb("par", [P, NROW + 2 * NCW])
        pool_bd = sb("pool_bd", [P, 2 * NPOOL, P])
        wr = sb("wr", [P, KD, E])
        wr_hi = sb("wr_hi", [P, KD, E], F32R)
        wr_lo = sb("wr_lo", [P, KD, E], F32R)
        small = sb("small", [P, 64])
        ident, ones = cst[:, C_ID:C_ID + P], cst[:, C_ONE:C_ONE + P]
        part = small[:, 32:36].rearrange("p (t c) -> p t c", t=NT)
        ss, rstd = small[:, 0:2], small[:, 2:4]
        sd = small[:, 4:6]
        eps_col = small[:, 6:7]
        top_neg, top_sum, top_inv = small[:, 8:16], small[:, 16:24], small[:, 24:32]

        dense = ctx.enter_context(ExitStack())
        kT = sb("kT", [P, KD, S], scope=dense)
        v = sb("v", [P, NT, D], scope=dense)
        hpad = sb("hpad", [P, NCONF, TAPS - 1 + S], scope=dense)
        upad = sb("upad", [P, NPOOL, 16 + S], scope=dense)
        win2 = sb("win2", [P, NPOOL, 16 + S], scope=dense)
        win4 = sb("win4", [P, NPOOL, 16 + S], scope=dense)
        win8 = sb("win8", [P, 16 + S], scope=dense)
        win16 = sb("win16", [P, 16 + S], scope=dense)
        spad = sb("spad", [P, NSC, SCTAPS - 1 + S], scope=dense)
        stat = sb("stat", [P, 8, S], scope=dense)
        mixer = dense.enter_context(ExitStack())
        z = sb("z", [P, NZ, S], scope=mixer)
        mixer.close()
        ffn = dense.enter_context(ExitStack())
        f_sil = [sb(f"f_sil{i}", [P, 512], scope=ffn) for i in range(2)]
        f_a = [sb(f"f_a{i}", [P, 512], scope=ffn) for i in range(2)]
        f_hi = [sb(f"f_hi{i}", [P, 512], F32R, scope=ffn) for i in range(2)]
        f_lo = [sb(f"f_lo{i}", [P, 512], F32R, scope=ffn) for i in range(2)]
        ffn.close()
        dense.close()
        moe = ctx.enter_context(ExitStack())
        xe_hi = sb("xe_hi", [P, KD, SLOTS], F32R, scope=moe)
        xe_lo = sb("xe_lo", [P, KD, SLOTS], F32R, scope=moe)
        y_hi = sb("y_hi", [P, D], F32R, scope=moe)
        y_lo = sb("y_lo", [P, D], F32R, scope=moe)
        sil = [sb(f"sil{i}", [P, 512], scope=moe) for i in range(2)]
        prod = [sb(f"prod{i}", [P, 512], scope=moe) for i in range(2)]
        a_hi = [sb(f"a_hi{i}", [P, 512], F32R, scope=moe) for i in range(2)]
        a_lo = [sb(f"a_lo{i}", [P, 512], F32R, scope=moe) for i in range(2)]
        pick = sb("pick", [P, NT, SLOTS], F32R, scope=moe)
        gpick = sb("gpick", [P, NT, SLOTS], scope=moe)
        place = sb("place", [P, S], F32R, scope=moe)
        rank = sb("rank", [P, NT, 2 * E + 1], scope=moe)
        gate = sb("gate", [P, NT, 2 * E + 1], scope=moe)
        best = sb("best", [P, NT, E], scope=moe)
        idx8 = sb("idx8", [P, NT, E], U32, scope=moe)
        idx = sb("idx", [P, NT, E], scope=moe)
        hot = sb("hot", [P, 2, NT, E], scope=moe)
        mask = sb("mask", [P, NT, E], scope=moe)
        slot1 = sb("slot1", [P, NT, E], scope=moe)
        diff = sb("diff", [P, NT, 1], scope=moe)
        ex = sb("ex", [P, NT, 1], scope=moe)
        gw = sb("gw", [P, 2, NT, 1], scope=moe)
        cnt = sb("cnt", [P, 2], scope=moe)
        rcol = sb("rcol", [P, NT, 1], scope=moe)
        gcol = sb("gcol", [P, NT, 1], scope=moe)
        gslot = sb("gslot", [P, 1], scope=moe)
        passes = sb("passes", [P, 1], I32, scope=moe)
        zero = sb("zero", [P, 512], scope=moe)

        bank = [ctx.enter_context(nc.psum_tensor(f"bank{i}", [P, 512], F32)) for i in range(8)]
        pair = ((bank[0], bank[1]), (bank[2], bank[3]))

        tok_hi = act_hi[:, :, :].rearrange("p k s -> p (k s)").rearrange("p (t d) -> p t d", t=NT)
        tok_lo = act_lo[:, :, :].rearrange("p k s -> p (k s)").rearrange("p (t d) -> p t d", t=NT)
        scr = xn[:, :, :].rearrange("p t d -> p (t d)").rearrange("p (b s) -> p b s", s=S)
        z_sq = scr

        raw_in = [sem(f"raw_in{i}") for i in range(RAW)]
        hi_done = sem("hi_done")
        lo_done = sem("lo_done")
        used = sem("used")
        pair_free = [sem(f"pair_free{i}") for i in range(2)]
        s_x = [sem(f"x_in{t}") for t in range(NT)]
        s_mem, s_cst, s_rows, s_wr, s_pw = (sem(n) for n in ("mem_in", "cst_in", "rows_in", "wr_in", "poolw_in"))
        squared, res_added = sem("squared"), sem("res_added")
        s_gain = sem("gain_in")
        eps_set = sem("eps_set")
        pads = sem("pads_zeroed")
        bd_zero = sem("pool_bd_zeroed")
        par_t = sem("par_transposed")
        par_c = sem("par_copied")
        norm_ss, norm_sd, norm_x = sem("norm_ss"), sem("norm_sd"), sem("norm_x")
        norm_t, norm_hi, norm_lo = sem("norm_t"), sem("norm_hi"), sem("norm_lo")
        mix_dve, mix_act, mix_pe, mix_pool = sem("mix_dve"), sem("mix_act"), sem("mix_pe"), sem("mix_pool")
        scores, top, probs, normed = sem("scores"), sem("top"), sem("probs"), sem("normed")
        pt, pt_even, pt_odd = sem("pt"), sem("pt_even_copied"), sem("pt_odd_copied")
        attn_o, o_hi, o_lo = sem("attn_o"), sem("o_hi"), sem("o_lo")
        f_silu, f_prod, f_ahi, f_alo = sem("f_silu"), sem("f_prod"), sem("f_ahi"), sem("f_alo")
        chain = sem("dve_chain")
        loop_chain = sem("dve_loop_chain")
        pchain = sem("pool_chain")
        wr_split = sem("wr_split")
        logits, masks, ranks, routed = sem("logits"), sem("masks"), sem("ranks"), sem("routed")
        margins, r_exp = sem("router_margins"), sem("router_exp")
        tok_split = sem("tok_split")
        picked, gpicked = sem("picked"), sem("gpicked")
        gathered, xe_hi_done, xe_lo_done = sem("gathered"), sem("xe_hi_done"), sem("xe_lo_done")
        placed_t, placed = sem("placed_t"), sem("placed")
        m_sil, m_prod, m_tr, m_ahi, m_alo = sem("m_sil"), sem("m_prod"), sem("m_tr"), sem("m_ahi"), sem("m_alo")
        y_hi_done, y_lo_done = sem("y_hi_done"), sem("y_lo_done")
        combined, added = sem("combined"), sem("added")
        s_out = sem("out_stored")

        def kn(w, rows0, nk, c0, n):
            return w[rows0:rows0 + nk * P, c0:c0 + n].rearrange("(k p) n -> p k n", p=P)

        def dense_stream():
            for layer in range(2):
                for b0, nb in WIN_CHUNKS[:-1]:
                    for half in range(2):
                        yield kn(w_in[layer], half * 512, 4, b0 * P, 512)
                yield kn(w_in[layer], 0, KD, 0, P)
                if layer == 0:
                    for c in range(4):
                        for half in range(2):
                            yield kn(w_mem_kv, half * 512, 4, c * 512, 512)
                for w in (w_out[layer], w_q[layer], w_o[layer]):
                    for c in range(2):
                        for half in range(2):
                            yield kn(w, half * 512, 4, c * 512, 512)
                if layer == 0:
                    down = [kn(w_down_dense[0], j * 256, 2, 0, D) for j in range(NF)]
                    for j in range(NF):
                        yield kn(w_gu_dense[0], 0, KD, j * 256, 256)
                        yield kn(w_gu_dense[0], 0, KD, FF + j * 256, 256)
                        if j:
                            yield down[j - 1]
                    yield down[NF - 1]

        def expert_pieces():
            out = []
            for c in range(CE):
                out += [("gate", c, 0), ("gate", c, 1), ("up", c, 0), ("up", c, 1)]
                if c:
                    out += [("down", c - 1, 0), ("down", c - 1, 1)]
            return out + [("down", CE - 1, 0), ("down", CE - 1, 1)]

        EP = expert_pieces()

        def expert_src(e, i):
            kind, c, half = EP[i]
            if kind == "down":
                w = w_down_moe[0, e, (c * 4 + half * 2) * P:(c * 4 + half * 2 + 2) * P, :]
                return w.rearrange("(k p) n -> p k n", p=P)
            c0 = c * 512 + (FE if kind == "up" else 0)
            return w_gu_moe[0, e, half * 512:half * 512 + 512, c0:c0 + 512].rearrange("(k p) n -> p k n", p=P)

        DENSE = list(dense_stream())
        SIZES = [s.shape[1] * s.shape[2] for s in DENSE]

        def load(sp, q, src, raw_free):
            nk, n = src.shape[1], src.shape[2]
            if raw_free is not None:
                sp.wait_ge(lo_done, raw_free)
            dst = raw[q % RAW][:, 0:nk * n].rearrange("p (k n) -> p k n", k=nk)
            sp.dma_start(dst, src).then_inc(raw_in[q % RAW], 16)

        def split_hi(act, q, n=PIECE, it=None):
            landed, left = 16 * (q // RAW + 1), q - SPLIT + 1
            if it is None:
                act.wait_ge(raw_in[q % RAW], landed)
                if left > 0:
                    act.wait_ge(used, left)
            else:
                act.wait_ge(raw_in[q % RAW], it * (16 * NE_PIECE // RAW) + landed)
                act.wait_ge(used, it * NE_PIECE + left)
            nc.scalar.activation(w_hi[q % SPLIT][:, 0:n], raw[q % RAW][:, 0:n], ACT.Copy).then_inc(hi_done, 1)

        def split_lo(dve, q, n=PIECE, it=None):
            dve.wait_ge(hi_done, q + 1 if it is None else it * NE_PIECE + (q + 1))
            nc.vector.tensor_tensor(w_lo[q % SPLIT][:, 0:n], raw[q % RAW][:, 0:n],
                                    w_hi[q % SPLIT][:, 0:n].bitcast(F32), ALU.subtract).then_inc(lo_done, 1)

        block = ctx.enter_context(nc.Block())

        @block.sync
        def _(sp):
            for t in range(NT):
                sp.dma_start(res[:, t, :], x[0, t * P:(t + 1) * P, :]).then_inc(s_x[t], 16)
            sp.wait_ge(s_gain, 16)
            for q, src in enumerate(DENSE):
                load(sp, q, src, q - RAW + 1 if q >= RAW else None)

            def expert_round(pass_pieces, e):
                for i in range(AHEAD, NE_PIECE):
                    load_expert(e, i, pass_pieces)
                nxt = (e + 1) % E
                for i in range(AHEAD):
                    load_expert(nxt, NE_PIECE + i, pass_pieces)

            def load_expert(e, i, before):
                sp.wait_ge(lo_done, before + (MOE0 + i - RAW + 1))
                q = MOE0 + i
                src = expert_src(e, i % NE_PIECE)
                dst = raw[q % RAW][:, :].rearrange("p (k n) -> p k n", k=src.shape[1])
                sp.dma_start(dst, src).then_inc(raw_in[q % RAW], 16)

            for i in range(AHEAD):
                load_expert(0, i, 0)
            with sp.Fori(0, E) as e:
                expert_round(e * NE_PIECE, e)
            sp.wait_ge(routed, 1)
            n_pass = sp.value_load(passes[0:1, 0:1], min_val=1, max_val=2)
            with sp.If(n_pass > 1):
                with sp.Fori(0, E) as e:
                    expert_round((e + E) * NE_PIECE, e)
            for t in range(NT):
                sp.wait_ge(norm_x, 4 * 7 + 3 + t)
                sp.dma_start(out[0, t * P:(t + 1) * P, :], xn[:, t, :]).then_inc(s_out, 16)
            sp.wait_ge(s_out, 16 * NT)

        @block.gpsimd
        def _(pool):
            gains = (mix_norm_g[0:1, :], mem_norm_g.rearrange("(a d) -> a d", a=1), xattn_norm_g[0:1, :],
                     ffn_norm_g[0:1, :], mix_norm_g[1:2, :], xattn_norm_g[1:2, :], ffn_norm_g[1:2, :],
                     final_norm_g.rearrange("(a d) -> a d", a=1))

            def load_gain(n):
                if n:
                    pool.wait_ge(norm_x, 4 * n)
                pool.dma_start(gain[:, :], gains[n].partition_broadcast(P)
                               if len(gains[n].shape) == 1 else gains[n].broadcast_to([P, D])).then_inc(s_gain, 16)

            load_gain(0)
            nc.gpsimd.memset(pool_bd[:, :, :], 0.0).then_inc(bd_zero, 1)
            for t in (hpad, upad, spad):
                last = nc.gpsimd.memset(t[:, :, :], 0.0)
            nc.gpsimd.memset(win2[:, :, :], 0.0)
            nc.gpsimd.memset(win4[:, :, :], 0.0)
            nc.gpsimd.memset(win8[:, :], 0.0)
            last = nc.gpsimd.memset(win16[:, :], 0.0)
            last.then_inc(pads, 1)
            pool.wait_ge(pads, 1)
            load_gain(1)
            steps = [0]

            def link(ins):
                steps[0] += 1
                ins.then_inc(pchain, 1)
                pool.wait_ge(pchain, steps[0])

            pool.wait_ge(s_cst, 16)
            for layer in range(2):
                if layer:
                    load_gain(5)
                n0 = BASE[layer]["win"][1]
                for n in (n0 + 3, n0 + 4):
                    pool.wait_ge(pair_free[n % 2], n // 2 + 1)
                H = 16
                link(nc.gpsimd.tensor_copy(upad[:, :, H:], z[:, 0:NPOOL, :]))
                link(nc.gpsimd.tensor_tensor(win2[:, :, H:], upad[:, :, H:], upad[:, :, H - 1:H - 1 + S], ALU.add))
                link(nc.gpsimd.tensor_tensor(win4[:, :, H:], win2[:, :, H:], win2[:, :, H - 2:H - 2 + S], ALU.add))
                link(nc.gpsimd.tensor_tensor(win8[:, H:], win4[:, 1, H:], win4[:, 1, H - 4:H - 4 + S], ALU.add))
                link(nc.gpsimd.tensor_tensor(win16[:, H:], win8[:, H:], win8[:, H - 8:H - 8 + S], ALU.add))
                inv = cst[:, C_INV:C_INV + 2 * S].rearrange("p (b s) -> p b s", b=2)
                h = P // 2
                for b, lo_w, hi_w in ((0, win2[0:h, 0, H:], win4[h:P, 0, H:]), (1, win8[0:h, H:], win16[h:P, H:])):
                    nc.gpsimd.tensor_tensor(z[0:h, b, :], lo_w, inv[0:h, b, :], ALU.mult)
                    link(nc.gpsimd.tensor_tensor(z[h:P, b, :], hi_w, inv[h:P, b, :], ALU.mult))
                nc.gpsimd.tensor_tensor(z[:, 0:NPOOL, :], z[:, 0:NPOOL, :], upad[:, :, H:],
                                        ALU.subtract).then_inc(mix_pool, 1)
                if layer == 0:
                    load_gain(2)
                    load_gain(3)
                    load_gain(4)
                else:
                    load_gain(6)
                    load_gain(7)

        @block.scalar
        def _(act):
            act.dma_start(cst[:, :], table).then_inc(s_cst, 16)
            act.dma_start(v[:, :, :], mem[0].rearrange("(t p) d -> p t d", p=P)).then_inc(s_mem, 16)
            for name, src in (("pool_scale", pool_scale), ("conf_b", conf_b), ("conf_ln_g", conf_ln_g),
                              ("conf_ln_b", conf_ln_b), ("group_norm_g", group_norm_g)):
                src = src.rearrange("l (b p) -> (l b) p", p=P)
                act.dma_start(rows[ROWS[name]:ROWS[name] + src.shape[0], 0, :], src).then_inc(s_rows, 16)
            src = sconv_w.rearrange("l k (b p) -> (l k b) p", p=P)
            act.dma_start(rows[ROWS["sconv_w"]:ROWS["sconv_w"] + src.shape[0], 0, :], src).then_inc(s_rows, 16)
            for layer in range(2):
                src = conf_w[layer].rearrange("k (b p) -> (k b) p", p=P)
                act.dma_start(rows[0:NCW, 1 + layer, :], src).then_inc(s_rows, 16)
            act.dma_start(wr[:, :, :], w_router[0].rearrange("(k p) e -> p k e", p=P)).then_inc(s_wr, 16)
            act.wait_ge(bd_zero, 1)
            for layer in range(2):
                for g in range(4):
                    h = P // 2 * (g % 2)
                    act.dma_start(pool_bd[h:h + P // 2, layer * NPOOL + g // 2, h:h + P // 2],
                                  pool_w[layer, g]).then_inc(s_pw, 16)
            qn = [0]

            def hi_upto(q):
                while qn[0] <= q and qn[0] < MOE0:
                    split_hi(act, qn[0], SIZES[qn[0]])
                    qn[0] += 1

            def norm(n, src=res, landed=None, done=False):
                for c in range(2):
                    if landed is None and not done:
                        act.wait_ge(res_added, 2 * (n - 2) + c + 1)
                    elif landed is not None and c == 0:
                        act.wait_ge(landed, 16)
                    cols = slice(c * 512, (c + 1) * 512)
                    nc.scalar.activation(xn[:, 0, cols], src[:, 0, cols], ACT.Square,
                                         accum_out=part[:, 0, c:c + 1]).then_inc(squared, 1)
                act.wait_ge(norm_ss, n + 1)
                nc.scalar.activation(sd, ss, ACT.Sqrt, scale=1.0 / D, bias=eps_col).then_inc(norm_sd, 1)

            def norm_split(n):
                for g in range(2):
                    for t in range(NT):
                        act.wait_ge(norm_t, 4 * n + 2 * g + t + 1)
                        nc.scalar.activation(act_hi[:, 4 * g:4 * g + 4, t * P:(t + 1) * P],
                                             bank[4 + 2 * g + t][:, :].rearrange("p (k s) -> p k s", k=4),
                                             ACT.Copy).then_inc(norm_hi, 1)

            act.wait_ge(eps_set, 1)
            norm(0, landed=s_x[0])
            for layer in range(2):
                q0, n0 = BASE[layer]["win"]
                norm_i = 0 if layer == 0 else 4
                if layer:
                    norm(4)
                norm_split(norm_i)
                for c, (b0, nb) in enumerate(WIN_CHUNKS):
                    n = n0 + c
                    last = q0 + (2 * c + 1 if c < 4 else 8)
                    hi_upto(last + AHEAD)
                    act.wait_ge(used, last + 1)
                    lo_bank, hi_bank = pair[n % 2]
                    if c == 0:
                        nc.scalar.activation(z[:, b0, :], lo_bank[:, 0:S], ACT.Copy)
                        nc.scalar.activation(z[:, b0 + 1, :], lo_bank[:, S:2 * S], ACT.Sigmoid)
                        nc.scalar.activation(z[:, b0 + 2:b0 + 4, :], hi_bank[:, :].rearrange("p (b s) -> p b s", s=S),
                                             ACT.Sigmoid).then_inc(pair_free[n % 2], 1)
                    elif nb == 4:
                        nc.scalar.activation(z[:, b0:b0 + 2, :], lo_bank[:, :].rearrange("p (b s) -> p b s", s=S),
                                             ACT.Copy)
                        nc.scalar.activation(z[:, b0 + 2:b0 + 4, :], hi_bank[:, :].rearrange("p (b s) -> p b s", s=S),
                                             ACT.Copy).then_inc(pair_free[n % 2], 1)
                    else:
                        nc.scalar.activation(z[:, b0, :], lo_bank[:, 0:S], ACT.Copy).then_inc(pair_free[n % 2], 1)
                    if layer == 0 and c == 0:
                        act.wait_ge(norm_t, 4)
                        norm(1, v, s_mem)
                if layer == 0:
                    norm_split(1)
                    q0, n0 = BASE[0]["kv"]
                    for c in range(4):
                        n = n0 + c
                        hi_upto(q0 + 2 * c + 1 + AHEAD)
                        act.wait_ge(used, q0 + 2 * c + 2)
                        if c < 2:
                            for i in range(2):
                                ins = nc.scalar.activation(kT[:, 4 * c + 2 * i:4 * c + 2 * i + 2, :],
                                                           pair[n % 2][i][:, :].rearrange("p (b s) -> p b s", s=S),
                                                           ACT.Copy)
                        else:
                            for t in range(NT):
                                ins = nc.scalar.activation(v[:, t, (c - 2) * 512:(c - 1) * 512], pair[n % 2][t][:, :],
                                                           ACT.Copy)
                        ins.then_inc(pair_free[n % 2], 1)
                conf = z[:, 11:14, :]

                def d(name):
                    act.wait_ge(mix_dve, step(MIX_DVE, name, layer))

                def pe_(name):
                    act.wait_ge(mix_pe, step(MIX_PE, name, layer))

                pe_("mean")
                nc.scalar.activation(stat[:, 0, :], bank[4][:, 0:S], ACT.Copy, scale=1.0 / 384).then_inc(mix_act, 1)
                d("centred")
                nc.scalar.activation(z_sq[:, 5:8, :], conf, ACT.Square).then_inc(mix_act, 1)
                pe_("var")
                nc.scalar.activation(stat[:, 1, :], bank[5][:, 0:S], ACT.Sqrt, scale=1.0 / 384,
                                     bias=eps_col).then_inc(mix_act, 1)
                d("scaled")
                for b in range(NCONF):
                    g = par[:, ROWS["conf_ln_g"] + layer * NCONF + b:ROWS["conf_ln_g"] + layer * NCONF + b + 1]
                    bb = par[:, ROWS["conf_ln_b"] + layer * NCONF + b:ROWS["conf_ln_b"] + layer * NCONF + b + 1]
                    ins = nc.scalar.activation(z[:, 11 + b, :], z[:, 11 + b, :], ACT.Silu, scale=g, bias=bb)
                ins.then_inc(mix_act, 1)
                d("pool_y")
                nc.scalar.activation(z_sq[:, 0:2, :], z[:, 0:2, :], ACT.Square).then_inc(mix_act, 1)
                pe_("pool_ssq")
                nc.scalar.activation(stat[:, 3, :], bank[7][:, 0:S], ACT.Sqrt, scale=1.0 / 256,
                                     bias=eps_col).then_inc(mix_act, 1)
                d("sconv_y")
                nc.scalar.activation(z_sq[:, 2:5, :], z[:, 2:5, :], ACT.Square).then_inc(mix_act, 1)
                pe_("sconv_ssq")
                nc.scalar.activation(stat[:, 4, :], bank[4][:, 0:S], ACT.Sqrt, scale=1.0 / 384,
                                     bias=eps_col).then_inc(mix_act, 1)
                nc.scalar.activation(z_sq[:, 5:8, :], conf, ACT.Square).then_inc(mix_act, 1)
                pe_("rms_ssq")
                nc.scalar.activation(stat[:, 5, :], bank[5][:, 0:S], ACT.Sqrt, scale=1.0 / 384,
                                     bias=eps_col).then_inc(mix_act, 1)
                for name, b0, b1, z0 in (("y_pool", 0, 2, 0), ("y_sconv", 2, 5, 2), ("y_conf", 5, 8, 11)):
                    d(name)
                    nc.scalar.activation(act_hi[:, b0:b1, :], z[:, z0:z0 + b1 - b0, :],
                                         ACT.Copy).then_inc(mix_act, 1)
                q0, n0 = BASE[layer]["wout"]
                hi_upto(q0 + N_SQ - 1 + AHEAD)
                norm_i += 2 if layer == 0 else 1
                norm(norm_i)
                norm_split(norm_i)
                q0, n0 = BASE[layer]["wq"]
                for c in range(2):
                    n = n0 + c
                    hi_upto(q0 + 2 * c + 1 + AHEAD)
                    act.wait_ge(used, q0 + 2 * c + 2)
                    for i in range(2):
                        ins = nc.scalar.activation(scr[:, 4 * c + 2 * i:4 * c + 2 * i + 2, :],
                                                   pair[n % 2][i][:, :].rearrange("p (b s) -> p b s", s=S), ACT.Copy)
                    ins.then_inc(pair_free[n % 2], 1)
                for h in range(HEADS):
                    act.wait_ge(top, layer * HEADS + h + 1)
                    for t in range(NT):
                        i = 2 * h + t
                        ins = nc.scalar.activation(z[:, i, :], bank[4 + h][:, t * S:(t + 1) * S], ACT.Exp,
                                                   scale=1.0 / 16, bias=top_neg[:, i:i + 1],
                                                   accum_out=top_sum[:, i:i + 1])
                    ins.then_inc(probs, 1)
                for h in range(0, HEADS, 2):
                    act.wait_ge(pt, layer * HEADS + h + 1)
                    nc.scalar.activation(z[:, 8 + 2 * h:10 + 2 * h, :],
                                         bank[4 + h][:, :].rearrange("p (b s) -> p b s", s=S),
                                         ACT.Copy).then_inc(pt_even, 1)
                for h in range(HEADS):
                    act.wait_ge(attn_o, layer * HEADS + h + 1)
                    nc.scalar.activation(act_hi[:, 2 * h:2 * h + 2, :],
                                         bank[4 + h][:, :].rearrange("p (b s) -> p b s", s=S),
                                         ACT.Copy).then_inc(o_hi, 1)
                q0, n0 = BASE[layer]["wo"]
                hi_upto(q0 + N_SQ - 1 + AHEAD)
                norm_i += 1
                norm(norm_i)
                norm_split(norm_i)
                if layer == 0:
                    q0, n0 = BASE[0]["ffn"]
                    for j in range(NF):
                        g = q0 + ffn_piece("gate", j)
                        hi_upto(g + AHEAD)
                        act.wait_ge(used, g + 1)
                        if j >= 2:
                            act.wait_ge(f_prod, j - 1)
                        nc.scalar.activation(f_sil[j % 2][:, :], pair[j % 2][0][:, :], ACT.Silu).then_inc(f_silu, 1)
                        hi_upto(g + 1 + AHEAD)
                        act.wait_ge(f_prod, j + 1)
                        if j >= 2:
                            act.wait_ge(used, q0 + ffn_piece("down", j - 2) + 1)
                        nc.scalar.activation(f_hi[j % 2][:, :], f_a[j % 2][:, :], ACT.Copy).then_inc(f_ahi, 1)
                    hi_upto(q0 + N_FFN - 1 + AHEAD)
            act.wait_ge(s_wr, 16)
            nc.scalar.activation(wr_hi[:, :, :], wr[:, :, :], ACT.Copy).then_inc(wr_split, 1)
            act.wait_ge(logits, NT)
            nc.scalar.activation(tok_hi[:, :, :], xn[:, :, :], ACT.Copy).then_inc(tok_split, 1)
            act.wait_ge(margins, 1)
            nc.scalar.activation(ex[:, :, :], diff[:, :, :], ACT.Exp).then_inc(r_exp, 1)
            for i in range(AHEAD):
                split_hi(act, MOE0 + i)

            def gather_hi(r):
                for b in range(2):
                    act.wait_ge(gathered, r * 2 + (b + 1))
                    nc.scalar.activation(xe_hi[:, 4 * b:4 * b + 4, :], pair[1][b][:, :].rearrange("p (k s) -> p k s", k=4),
                                         ACT.Copy).then_inc(xe_hi_done, 1)

            gather_hi(0)
            act.wait_ge(routed, 1)
            n_pass = act.value_load(passes[0:1, 0:1], min_val=1, max_val=2)
            with act.Fori(0, n_pass) as ps:
                with act.Fori(0, E) as e:
                    it = ps * E + e
                    before = it * NE_PIECE

                    def hi(i0, i1):
                        for i in range(i0, i1):
                            split_hi(act, MOE0 + i, it=it)

                    def silu(c):
                        act.wait_ge(used, before + (MOE0 + (0 if c == 0 else 6 * c - 2) + 2))
                        nc.scalar.activation(sil[c % 2][:, :], pair[c % 2][0][:, :], ACT.Silu).then_inc(m_sil, 1)

                    def a_split(c):
                        act.wait_ge(m_tr, it * CE + (c + 1))
                        if c >= 2:
                            act.wait_ge(used, before + (MOE0 + 6 * (c - 1) + 4))
                        else:
                            act.wait_ge(used, before + MOE0)
                        nc.scalar.activation(a_hi[c % 2][:, :], bank[6 + c % 2][:, :], ACT.Copy).then_inc(m_ahi, 1)

                    hi(2, 4)
                    silu(0)
                    for c in range(1, CE):
                        b = 6 * c - 2
                        hi(b - 2 if c > 1 else 4, b + 4)
                        silu(c)
                        a_split(c - 1)
                    hi(6 * CE - 4, 6 * CE)
                    a_split(CE - 1)
                    gather_hi(it + 1)
                    hi(NE_PIECE, NE_PIECE + AHEAD)
                    act.wait_ge(used, before + (MOE0 + NE_PIECE))
                    for b in range(2):
                        nc.scalar.activation(y_hi[:, b * 512:(b + 1) * 512], bank[4 + b][:, :], ACT.Copy,
                                             scale=gslot[:, 0:1]).then_inc(y_hi_done, 1)
            act.wait_ge(added, n_pass * (4 * E) + 4)
            norm(7, done=True)

        @block.vector
        def _(dve):
            steps = [0]

            def done(ins):
                steps[0] += 1
                ins.then_inc(chain, 1)
                return steps[0]

            def link(ins):
                dve.wait_ge(chain, done(ins))

            qn = [0]

            def lo_upto(q):
                while qn[0] <= q and qn[0] < MOE0:
                    split_lo(dve, qn[0], SIZES[qn[0]])
                    qn[0] += 1

            def square(src, c):
                cols = slice(c * 512, (c + 1) * 512)
                return done(nc.vector.tensor_tensor_reduce(out=xn[:, 1, cols], in0=src[:, 1, cols], in1=src[:, 1, cols],
                                                           scale=1.0, scalar=0.0, op0=ALU.mult, op1=ALU.add,
                                                           accum_out=part[:, 1, c:c + 1]))

            def norm(n, src=res, landed=None):
                if landed is not None:
                    dve.wait_ge(landed, 16)
                    for c in range(2):
                        last = square(src, c)
                    dve.wait_ge(chain, last)
                dve.wait_ge(squared, 2 * n + 2)
                nc.vector.tensor_tensor(ss, part[:, :, 0], part[:, :, 1], ALU.add).then_inc(norm_ss, 1)
                dve.wait_ge(norm_sd, n + 1)
                link(nc.vector.reciprocal(rstd, sd))
                dve.wait_ge(s_gain, 16 * (n + 1))
                for c in range(2):
                    cols = slice(c * 512, (c + 1) * 512)
                    for t in range(NT):
                        nc.vector.scalar_tensor_tensor(out=xn[:, t, cols], in0=src[:, t, cols], scalar=rstd[:, t:t + 1],
                                                       in1=gain[:, cols], op0=ALU.mult,
                                                       op1=ALU.mult).then_inc(norm_x, 1)

            def norm_split(n):
                for g in range(2):
                    for t in range(NT):
                        i = 2 * g + t
                        dve.wait_ge(norm_hi, 4 * n + i + 1)
                        dst = act_lo[:, 4 * g:4 * g + 4, t * P:(t + 1) * P]
                        nc.vector.tensor_tensor(dst, bank[4 + i][:, :].rearrange("p (k s) -> p k s", k=4),
                                                act_hi[:, 4 * g:4 * g + 4, t * P:(t + 1) * P].bitcast(F32),
                                                ALU.subtract).then_inc(norm_lo, 1)

            def chunk_out(n):
                dve.wait_ge(pair_free[n % 2], n // 2 + 1)

            def add_half(c, banks):
                cols = slice(c * 512, (c + 1) * 512)
                nc.vector.tensor_tensor(res[:, 0, cols], banks[0][:, :], res[:, 0, cols], ALU.add).then_inc(res_added, 1)
                return nc.vector.tensor_tensor(res[:, 1, cols], banks[1][:, :], res[:, 1, cols], ALU.add)

            def add_chunks(q0, n0):
                for c in range(2):
                    n = n0 + c
                    lo_upto(q0 + 2 * c + 1 + AHEAD)
                    dve.wait_ge(used, q0 + 2 * c + 2)
                    add_half(c, pair[n % 2]).then_inc(pair_free[n % 2], 1)
                    dve.wait_ge(pair_free[n % 2], n // 2 + 1)
                    last = square(res, c)
                dve.wait_ge(chain, last)

            nc.vector.memset(eps_col, EPS).then_inc(eps_set, 1)
            dve.wait_ge(s_x[1], 16)
            norm(0, landed=s_x[0])
            norm_split(0)
            for layer in range(2):
                conf = z[:, 11:14, :]
                q0, n0 = BASE[layer]["win"]
                norm_i = 0
                if layer:
                    norm_i = 4
                    norm(4)
                    norm_split(4)
                lo_upto(q0 + 1 + AHEAD)
                if layer == 0:
                    norm(1, v, s_mem)
                    dve.wait_ge(par_t, 1)
                    nc.vector.tensor_copy(par[:, 0:NROW], bank[4][:, 0:NROW])
                    nc.vector.tensor_copy(par[:, NROW:NROW + NCW], bank[4][:, P:P + NCW])
                    nc.vector.tensor_copy(par[:, NROW + NCW:], bank[4][:, 2 * P:2 * P + NCW]).then_inc(par_c, 1)
                lo_upto(q0 + 3 + AHEAD)
                chunk_out(n0)
                chunk_out(n0 + 1)
                dve.wait_ge(pads, 1)
                dve.wait_ge(par_c, 1)
                ins = nc.vector.tensor_tensor(hpad[:, :, TAPS - 1:], conf, z[:, 14:17, :], ALU.mult)
                ins.then_inc(mix_dve, 1)
                dve.wait_ge(mix_dve, step(MIX_DVE, "prod", layer))

                def conv_taps():
                    for k in range(TAPS):
                        for b in range(NCONF):
                            acc = z[:, 11 + b, :]
                            src = hpad[:, b, k:k + S]
                            col = NROW + layer * NCW + k * NCONF + b
                            w = par[:, col:col + 1]
                            if k == 0:
                                cb = ROWS["conf_b"] + layer * NCONF + b
                                ins = nc.vector.tensor_scalar(acc, src, w, par[:, cb:cb + 1], ALU.mult, ALU.add)
                            else:
                                dve.wait_ge(chain, conv_at[b])
                                ins = nc.vector.scalar_tensor_tensor(out=acc, in0=src, scalar=w, in1=acc,
                                                                     op0=ALU.mult, op1=ALU.add)
                            if (k, b) == (TAPS - 1, NCONF - 1):
                                ins.then_inc(mix_dve, 1)
                            else:
                                conv_at[b] = done(ins)
                            yield

                conv_at = [0] * NCONF
                taps = conv_taps()

                def some_taps(n):
                    for _ in range(n):
                        next(taps, None)

                def pieces_with_taps(first, last):
                    for q in range(first, last + 1):
                        lo_upto(q + AHEAD)
                        some_taps(8)

                pieces_with_taps(q0 + 4, q0 + 8)
                if layer == 0:
                    norm_split(1)
                    q1, n1 = BASE[0]["kv"]
                    pieces_with_taps(q1, q1 + N_KV - 1)
                some_taps(TAPS * NCONF)
                for n in (n0 + 2, n0 + 3, n0 + 4):
                    chunk_out(n)
                link(nc.vector.tensor_tensor(spad[:, :, SCTAPS - 1:], z[:, 8:11, :], z[:, 2:5, :], ALU.mult))
                sc_at = [0] * NSC
                for k in range(SCTAPS):
                    for b in range(NSC):
                        acc = z[:, 2 + b, :]
                        col = ROWS["sconv_w"] + (layer * SCTAPS + k) * NSC + b
                        w = par[:, col:col + 1]
                        if k == 0:
                            ins = nc.vector.tensor_scalar(acc, spad[:, b, k:k + S], w, None, ALU.mult)
                        else:
                            dve.wait_ge(chain, sc_at[b])
                            ins = nc.vector.scalar_tensor_tensor(out=acc, in0=spad[:, b, k:k + S], scalar=w, in1=acc,
                                                                 op0=ALU.mult, op1=ALU.add)
                        sc_at[b] = done(ins)
                dve.wait_ge(chain, sc_at[-1])
                nc.vector.tensor_tensor(z[:, 2:5, :], z[:, 2:5, :], z[:, 5:8, :], ALU.mult).then_inc(mix_dve, 1)

                def a(name):
                    dve.wait_ge(mix_act, step(MIX_ACT, name, layer))

                a("mean")
                nc.vector.tensor_tensor(conf, conf, stat[:, 0:1, :].broadcast_to([P, NCONF, S]),
                                        ALU.subtract).then_inc(mix_dve, 1)
                a("conf_sd")
                link(nc.vector.reciprocal(stat[:, 2, :], stat[:, 1, :]))
                nc.vector.tensor_tensor(conf, conf, stat[:, 2:3, :].broadcast_to([P, NCONF, S]),
                                        ALU.mult).then_inc(mix_dve, 1)
                dve.wait_ge(mix_pe, step(MIX_PE, "pool", layer))
                for b in range(NPOOL):
                    c = ROWS["pool_scale"] + layer * NPOOL + b
                    ins = nc.vector.tensor_scalar(z[:, b, :], bank[6][:, b * S:(b + 1) * S], par[:, c:c + 1], None,
                                                  ALU.mult)
                ins.then_inc(mix_dve, 1)
                for sd_name, row, blocks in (("pool_sd", 3, ((0, 0), (1, 1))),
                                             ("sconv_sd", 4, ((2, 2), (3, 3), (4, 4))),
                                             ("rms_sd", 5, ((5, 11), (6, 12), (7, 13)))):
                    a(sd_name)
                    link(nc.vector.reciprocal(stat[:, row, :], stat[:, row, :]))
                    for k, zb in blocks:
                        c = ROWS["group_norm_g"] + layer * KD + k
                        ins = nc.vector.scalar_tensor_tensor(out=z[:, zb, :], in0=z[:, zb, :], scalar=par[:, c:c + 1],
                                                             in1=stat[:, row, :], op0=ALU.mult, op1=ALU.mult)
                    ins.then_inc(mix_dve, 1)
                for name, b0, b1, z0 in (("hi_pool", 0, 2, 0), ("hi_sconv", 2, 5, 2), ("hi_conf", 5, 8, 11)):
                    a(name)
                    nc.vector.tensor_tensor(act_lo[:, b0:b1, :], z[:, z0:z0 + b1 - b0, :],
                                            act_hi[:, b0:b1, :].bitcast(F32), ALU.subtract).then_inc(mix_dve, 1)
                add_chunks(*BASE[layer]["wout"])
                norm_i += 2 if layer == 0 else 1
                norm(norm_i)
                norm_split(norm_i)
                lo_upto(BASE[layer]["wq"][0] + N_SQ - 1 + AHEAD)
                for h in range(HEADS):
                    dve.wait_ge(scores, layer * HEADS + h + 1)
                    link(nc.vector.tensor_reduce(top_sum[:, 2 * h:2 * h + 2],
                                                 bank[4 + h][:, :].rearrange("p (t s) -> p t s", t=NT), AX.X, ALU.max))
                    nc.vector.tensor_scalar(top_neg[:, 2 * h:2 * h + 2], top_sum[:, 2 * h:2 * h + 2], -1.0 / 16, None,
                                            ALU.mult).then_inc(top, 1)
                for h in range(HEADS):
                    dve.wait_ge(probs, layer * HEADS + h + 1)
                    link(nc.vector.reciprocal(top_inv[:, 2 * h:2 * h + 2], top_sum[:, 2 * h:2 * h + 2]))
                    for t in range(NT):
                        i = 2 * h + t
                        ins = nc.vector.tensor_scalar(z[:, i, :], z[:, i, :], top_inv[:, i:i + 1], None, ALU.mult)
                    ins.then_inc(normed, 1)
                for h in range(1, HEADS, 2):
                    dve.wait_ge(pt, layer * HEADS + h + 1)
                    nc.vector.tensor_copy(z[:, 8 + 2 * h:10 + 2 * h, :],
                                          bank[4 + h][:, :].rearrange("p (b s) -> p b s", s=S)).then_inc(pt_odd, 1)
                for h in range(HEADS):
                    dve.wait_ge(o_hi, layer * HEADS + h + 1)
                    nc.vector.tensor_tensor(act_lo[:, 2 * h:2 * h + 2, :],
                                            bank[4 + h][:, :].rearrange("p (b s) -> p b s", s=S),
                                            act_hi[:, 2 * h:2 * h + 2, :].bitcast(F32), ALU.subtract).then_inc(o_lo, 1)
                add_chunks(*BASE[layer]["wo"])
                norm_i += 1
                norm(norm_i)
                norm_split(norm_i)
                if layer == 0:
                    q0, n0 = BASE[0]["ffn"]
                    for j in range(NF):
                        lo_upto(q0 + ffn_piece("up", j) + AHEAD)
                        dve.wait_ge(used, q0 + ffn_piece("up", j) + 1)
                        dve.wait_ge(f_silu, j + 1)
                        if j >= 2:
                            dve.wait_ge(f_ahi, j - 1)
                        ins = nc.vector.tensor_tensor(f_a[j % 2][:, :], pair[j % 2][1][:, :], f_sil[j % 2][:, :], ALU.mult)
                        ins.then_inc(f_prod, 1)
                        dve.wait_ge(f_ahi, j + 1)
                        nc.vector.tensor_tensor(f_lo[j % 2][:, :], f_a[j % 2][:, :], f_hi[j % 2][:, :].bitcast(F32),
                                                ALU.subtract).then_inc(f_alo, 1)
                    lo_upto(q0 + N_FFN - 1 + AHEAD)
                    dve.wait_ge(used, q0 + N_FFN)
                    for c in range(2):
                        link(add_half(c, (bank[4 + c], bank[6 + c])))
                        last = square(res, c)
                    dve.wait_ge(chain, last)
            dve.wait_ge(wr_split, 1)
            nc.vector.tensor_tensor(wr_lo[:, :, :], wr[:, :, :], wr_hi[:, :, :].bitcast(F32),
                                    ALU.subtract).then_inc(wr_split, 1)
            dve.wait_ge(logits, NT)
            for t in range(NT):
                last = done(nc.vector.max(best[:, t, :], bank[4 + t][:, 0:E]))
            dve.wait_ge(chain, last)
            for t in range(NT):
                last = done(nc.vector.max_index(idx8[:, t, :], best[:, t, :], bank[4 + t][:, 0:E]))
            nc.vector.tensor_tensor(diff[:, :, :], best[:, :, 1:2], best[:, :, 0:1],
                                    ALU.subtract).then_inc(margins, 1)
            dve.wait_ge(chain, last)
            link(nc.vector.tensor_copy(idx[:, :, :], idx8[:, :, :]))
            iota8 = cst[:, C_IOTA8:C_IOTA8 + E].rearrange("p (a e) -> p a e", a=1).broadcast_to([P, NT, E])
            for j in range(2):
                last = done(nc.vector.tensor_tensor(hot[:, j, :, :], idx[:, :, j:j + 1].broadcast_to([P, NT, E]), iota8,
                                                    ALU.is_equal))
            dve.wait_ge(chain, last)
            nc.vector.tensor_tensor(mask[:, :, :], hot[:, 0, :, :], hot[:, 1, :, :], ALU.add).then_inc(masks, 1)
            dve.wait_ge(tok_split, 1)
            nc.vector.tensor_tensor(tok_lo[:, :, :], xn[:, :, :], tok_hi[:, :, :].bitcast(F32),
                                    ALU.subtract).then_inc(tok_split, 1)
            dve.wait_ge(ranks, 1)
            link(nc.vector.scalar_tensor_tensor(out=slot1[:, :, :],
                                                in0=bank[6][:, 0:NT * E].rearrange("p (t e) -> p t e", t=NT),
                                                scalar=1.0, in1=mask[:, :, :], op0=ALU.add, op1=ALU.mult))
            nc.vector.tensor_scalar(rank[:, :, E:2 * E], slot1[:, :, :], float(SLOTS + 1), None, ALU.subtract)
            nc.vector.memset(rank[:, :, 2 * E:], -1.0)
            link(nc.vector.tensor_scalar(rank[:, :, 0:E], slot1[:, :, :], -1.0, None, ALU.add))
            iota = cst[:, C_IOTA:C_IOTA + SLOTS]
            link(nc.vector.tensor_copy(rcol[:, :, :], rank[:, :, 0:1]))
            for t in range(NT):
                ins = nc.vector.tensor_scalar(pick[:, t, :], iota, rcol[:, t, :], None, ALU.is_equal)
            ins.then_inc(picked, 1)
            link(nc.vector.tensor_reduce(cnt[:, 0:1], bank[6][:, NT * E:(NT + 1) * E], AX.X, ALU.max))
            link(nc.vector.tensor_scalar(cnt[:, 1:2], cnt[:, 0:1], float(SLOTS), 1.0, ALU.is_gt, ALU.add))
            nc.vector.tensor_copy(passes[:, :], cnt[:, 1:2]).then_inc(routed, 1)
            for i in range(AHEAD):
                split_lo(dve, MOE0 + i)
            dve.wait_ge(r_exp, 1)
            link(nc.vector.tensor_scalar(gw[:, 1, :, :], ex[:, :, :], 1.0, None, ALU.add))
            link(nc.vector.reciprocal(gw[:, 0, :, :], gw[:, 1, :, :]))
            link(nc.vector.tensor_tensor(gw[:, 1, :, :], ex[:, :, :], gw[:, 0, :, :], ALU.mult))
            for j in range(2):
                last = done(nc.vector.tensor_tensor(hot[:, j, :, :], hot[:, j, :, :],
                                                    gw[:, j, :, :].broadcast_to([P, NT, E]), ALU.mult))
            dve.wait_ge(chain, last)
            for half in range(2):
                nc.vector.tensor_tensor(gate[:, :, half * E:(half + 1) * E], hot[:, 0, :, :], hot[:, 1, :, :], ALU.add)
            nc.vector.memset(gate[:, :, 2 * E:], 0.0)

            def gather_lo(r):
                for b in range(2):
                    dve.wait_ge(xe_hi_done, r * 2 + (b + 1))
                    nc.vector.tensor_tensor(xe_lo[:, 4 * b:4 * b + 4, :],
                                            pair[1][b][:, :].rearrange("p (k s) -> p k s", k=4),
                                            xe_hi[:, 4 * b:4 * b + 4, :].bitcast(F32), ALU.subtract).then_inc(xe_lo_done, 1)

            gather_lo(0)
            link(nc.vector.memset(zero[:, :], 0.0))
            for b in range(2):
                nc.vector.tensor_copy(y_hi[:, b * 512:(b + 1) * 512], zero[:, 0:512])
                nc.vector.tensor_copy(y_lo[:, b * 512:(b + 1) * 512], zero[:, 0:512]).then_inc(y_lo_done, 1)
            nc.vector.tensor_copy(place[:, :], zero[:, 0:S]).then_inc(placed, 1)
            def add_combined(r, t):
                for b in range(2):
                    dve.wait_ge(combined, r * 4 + (2 * t + b + 1))
                    cols = res[:, t, b * 512:(b + 1) * 512]
                    nc.vector.tensor_tensor(cols, bank[6 + b][:, :], cols, ALU.add).then_inc(added, 1)

            dve.wait_ge(routed, 1)
            n_pass = dve.value_load(passes[0:1, 0:1], min_val=1, max_val=2)
            own = 2
            with dve.Fori(0, n_pass) as ps:
                with dve.Fori(0, E) as e:
                    it = ps * E + e
                    before = it * NE_PIECE

                    def lo(i0, i1):
                        for i in range(i0, i1):
                            split_lo(dve, MOE0 + i, it=it)

                    def product(c):
                        dve.wait_ge(used, before + (MOE0 + (0 if c == 0 else 6 * c - 2) + 4))
                        dve.wait_ge(m_sil, it * CE + (c + 1))
                        nc.vector.tensor_tensor(prod[c % 2][:, :], pair[c % 2][1][:, :], sil[c % 2][:, :],
                                                ALU.mult).then_inc(m_prod, 1)

                    def a_split(c):
                        dve.wait_ge(m_ahi, it * CE + (c + 1))
                        nc.vector.tensor_tensor(a_lo[c % 2][:, :], bank[6 + c % 2][:, :], a_hi[c % 2][:, :].bitcast(F32),
                                                ALU.subtract).then_inc(m_alo, 1)

                    def own_wait(k):
                        dve.wait_ge(loop_chain, it * own + k)

                    lo(2, 4)
                    add_combined(it, 0)
                    lo(4, 6)
                    add_combined(it, 1)
                    product(0)
                    nc.vector.tensor_copy(gcol[:, :, :], gate[:, :, bass.ds(it, 1)]).then_inc(loop_chain, 1)
                    nc.vector.tensor_copy(rcol[:, :, :], rank[:, :, bass.ds(it + 1, 1)]).then_inc(loop_chain, 1)
                    own_wait(2)
                    for t in range(NT):
                        ins = nc.vector.tensor_scalar(gpick[:, t, :], pick[:, t, :].bitcast(F32), gcol[:, t, :], None,
                                                      ALU.mult)
                    ins.then_inc(gpicked, 1)
                    dve.wait_ge(gpicked, it + 1)
                    for t in range(NT):
                        ins = nc.vector.tensor_scalar(pick[:, t, :], iota, rcol[:, t, :], None, ALU.is_equal)
                    ins.then_inc(picked, 1)
                    lo(6, 8)
                    a_split(0)
                    lo(8, 10)
                    product(1)
                    lo(10, 12)
                    dve.wait_ge(placed_t, it + 1)
                    nc.vector.tensor_reduce(gslot[:, :], bank[7][:, 0:S], AX.X, ALU.add)
                    nc.vector.tensor_scalar(place[:, :], bank[7][:, 0:S], 0.0, None, ALU.is_gt).then_inc(placed, 1)
                    for c in range(2, CE):
                        b = 6 * c - 2
                        lo(b + 2, b + 4)
                        a_split(c - 1)
                        lo(b + 4, b + 6)
                        product(c)
                        if c < CE - 1:
                            lo(b + 6, b + 8)
                    lo(6 * CE - 2, 6 * CE)
                    a_split(CE - 1)
                    gather_lo(it + 1)
                    lo(NE_PIECE, NE_PIECE + AHEAD)
                    for b in range(2):
                        dve.wait_ge(y_hi_done, it * 2 + (b + 1))
                        cols = slice(b * 512, (b + 1) * 512)
                        nc.vector.scalar_tensor_tensor(out=y_lo[:, cols], in0=bank[4 + b][:, :], scalar=gslot[:, 0:1],
                                                       in1=y_hi[:, cols].bitcast(F32), op0=ALU.mult,
                                                       op1=ALU.subtract).then_inc(y_lo_done, 1)
            rounds = n_pass * E
            add_combined(rounds, 0)
            add_combined(rounds, 1)
            dve.wait_ge(added, rounds * 4 + 4)
            for c in range(2):
                last = square(res, c)
            dve.wait_ge(chain, last)
            norm(7)

        @block.tensor
        def _(pe):
            mm = nc.tensor.matmul

            def norm_transpose(n):
                for g in range(2):
                    for t in range(NT):
                        pe.wait_ge(norm_x, 4 * n + 2 * g + t + 1)
                        for k in range(4):
                            kk = 4 * g + k
                            ins = nc.tensor.transpose(bank[4 + 2 * g + t][:, k * P:(k + 1) * P],
                                                      xn[:, t, kk * P:(kk + 1) * P], ident)
                        ins.then_inc(norm_t, 1)

            def take(q, nk, it=None):
                pe.wait_ge(lo_done, q + 1 if it is None else it * NE_PIECE + (q + 1))
                n = (SIZES[q] if q < MOE0 else PIECE) // nk
                return [w[q % SPLIT][:, 0:nk * n].rearrange("p (k n) -> p k n", k=nk) for w in (w_hi, w_lo)]

            def columns(q, banks, k0, nk, nb, first, last):
                hi, lo = take(q, nk)
                for b in range(nb):
                    dst = banks[b // 2][:, (b % 2) * S:(b % 2) * S + S]
                    cols = slice(b * P, (b + 1) * P)
                    for k in range(nk):
                        begin = first and k == 0 and b % 2 == 0
                        end = last and k == nk - 1
                        mm(dst, hi[:, k, cols], act_hi[:, k0 + k, :], start=begin, stop=False, skip_group_check=True)
                        mm(dst, hi[:, k, cols], act_lo[:, k0 + k, :], start=False, stop=False, skip_group_check=True)
                        ins = mm(dst, lo[:, k, cols], act_hi[:, k0 + k, :], start=False, stop=end,
                                 skip_group_check=True)
                ins.then_inc(used, 1)

            def tokens(q, banks, k0, first, last):
                hi, lo = take(q, 4)
                for t in range(NT):
                    for k in range(4):
                        ah, al = (x_[:, k0 + k, t * P:(t + 1) * P] for x_ in (act_hi, act_lo))
                        mm(banks[t][:, :], ah, hi[:, k, :], start=first and k == 0, stop=False)
                        mm(banks[t][:, :], ah, lo[:, k, :], start=False, stop=False)
                        ins = mm(banks[t][:, :], al, hi[:, k, :], start=False, stop=last and k == 3)
                ins.then_inc(used, 1)

            def free_pair(n):
                if n >= 2:
                    pe.wait_ge(pair_free[n % 2], n // 2)

            def product(q0, n0, chunks, how, norm_i=None):
                for c in range(chunks):
                    n = n0 + c
                    free_pair(n)
                    for half in range(2):
                        q = q0 + 2 * c + half
                        if norm_i is not None and c == 0:
                            pe.wait_ge(norm_lo, 4 * norm_i + 2 * half + 2)
                        if how == "columns":
                            columns(q, pair[n % 2], 4 * half, 4, 4, half == 0, half == 1)
                        else:
                            tokens(q, pair[n % 2], 4 * half, half == 0, half == 1)

            pe.wait_ge(s_cst, 16)
            norm_transpose(0)
            for layer in range(2):
                norm_i = 0 if layer == 0 else 4
                if layer:
                    norm_transpose(4)
                q0, n0 = BASE[layer]["win"]
                product(q0, n0, 1, "columns", norm_i)
                if layer == 0:
                    pe.wait_ge(s_rows, 16 * 8)
                    nc.tensor.transpose(bank[4][:, 0:NROW], rows[0:NROW, 0, :], ident[0:NROW, 0:NROW])
                    nc.tensor.transpose(bank[4][:, P:P + NCW], rows[0:NCW, 1, :], ident[0:NCW, 0:NCW])
                    nc.tensor.transpose(bank[4][:, 2 * P:2 * P + NCW], rows[0:NCW, 2, :],
                                        ident[0:NCW, 0:NCW]).then_inc(par_t, 1)
                product(q0 + 2, n0 + 1, 3, "columns")
                free_pair(n0 + 4)
                columns(q0 + 8, pair[(n0 + 4) % 2], 0, KD, 1, True, True)
                if layer == 0:
                    pe.wait_ge(par_c, 1)
                    norm_transpose(1)
                    q1, n1 = BASE[0]["kv"]
                    product(q1, n1, 2, "columns", 1)
                    product(q1 + 4, n1 + 2, 2, "tokens")

                def col_sum(dst, src, blocks):
                    for i, b in enumerate(blocks):
                        ins = mm(dst, ones, src[:, b, :], start=i == 0, stop=i == len(blocks) - 1)
                    ins.then_inc(mix_pe, 1)

                pe.wait_ge(mix_dve, step(MIX_DVE, "conv", layer))
                col_sum(bank[4][:, 0:S], z, (11, 12, 13))
                pe.wait_ge(mix_act, step(MIX_ACT, "conf_sq", layer))
                col_sum(bank[5][:, 0:S], z_sq, (5, 6, 7))
                pe.wait_ge(mix_pool, layer + 1)
                pe.wait_ge(s_pw, 16 * 8)
                for b in range(NPOOL):
                    ins = mm(bank[6][:, b * S:(b + 1) * S], pool_bd[:, layer * NPOOL + b, :], z[:, b, :],
                             start=True, stop=True)
                ins.then_inc(mix_pe, 1)
                pe.wait_ge(mix_act, step(MIX_ACT, "pool_sq", layer))
                col_sum(bank[7][:, 0:S], z_sq, (0, 1))
                pe.wait_ge(mix_act, step(MIX_ACT, "sconv_sq", layer))
                col_sum(bank[4][:, 0:S], z_sq, (2, 3, 4))
                pe.wait_ge(mix_act, step(MIX_ACT, "rms_sq", layer))
                col_sum(bank[5][:, 0:S], z_sq, (5, 6, 7))
                pe.wait_ge(mix_dve, step(MIX_DVE, "lo_conf", layer))
                product(*BASE[layer]["wout"], 2, "tokens")
                norm_i += 2 if layer == 0 else 1
                norm_transpose(norm_i)
                q0, n0 = BASE[layer]["wq"]
                product(q0, n0, 2, "columns", norm_i)
                for n in (n0, n0 + 1):
                    pe.wait_ge(pair_free[n % 2], n // 2 + 1)
                for h in range(HEADS):
                    for t in range(NT):
                        for b in range(2):
                            k = 2 * h + b
                            ins = mm(bank[4 + h][:, t * S:(t + 1) * S], scr[:, k, t * P:(t + 1) * P], kT[:, k, :],
                                     start=b == 0, stop=b == 1)
                    ins.then_inc(scores, 1)
                for h in range(HEADS):
                    pe.wait_ge(normed, layer * HEADS + h + 1)
                    for mb in range(NT):
                        for t in range(NT):
                            ins = nc.tensor.transpose(bank[4 + h][:, mb * S + t * P:mb * S + (t + 1) * P],
                                                      z[:, 2 * h + t, mb * P:(mb + 1) * P], ident)
                    ins.then_inc(pt, 1)
                for h in range(HEADS):
                    pe.wait_ge(pt_odd if h % 2 else pt_even, layer * 2 + h // 2 + 1)
                    for b in range(2):
                        for mb in range(NT):
                            ins = mm(bank[4 + h][:, b * S:(b + 1) * S], v[:, mb, (2 * h + b) * P:(2 * h + b + 1) * P],
                                     z[:, 8 + 2 * h + mb, :], start=mb == 0, stop=mb == NT - 1)
                    ins.then_inc(attn_o, 1)
                pe.wait_ge(o_lo, (layer + 1) * HEADS)
                product(*BASE[layer]["wo"], 2, "tokens")
                norm_i += 1
                norm_transpose(norm_i)
                pe.wait_ge(norm_lo, 4 * (norm_i + 1))
                if layer == 0:
                    q0, n0 = BASE[0]["ffn"]

                    def down(j):
                        hi, lo = take(q0 + ffn_piece("down", j), 2)
                        pe.wait_ge(f_alo, j + 1)
                        for b in range(2):
                            for t in range(NT):
                                cols = slice(b * S + t * P, b * S + (t + 1) * P)
                                ah, al = f_hi[j % 2][:, cols], f_lo[j % 2][:, cols]
                                for c in range(2):
                                    dst = bank[4 + 2 * t + c][:, :]
                                    w = slice(c * 512, (c + 1) * 512)
                                    begin, end = j == 0 and b == 0, j == NF - 1 and b == 1
                                    mm(dst, ah, hi[:, b, w], start=begin, stop=False)
                                    mm(dst, ah, lo[:, b, w], start=False, stop=False)
                                    ins = mm(dst, al, hi[:, b, w], start=False, stop=end)
                        ins.then_inc(used, 1)

                    for j in range(NF):
                        if j >= 2:
                            pe.wait_ge(f_prod, j - 1)
                        columns(q0 + ffn_piece("gate", j), (pair[j % 2][0],), 0, KD, 2, True, True)
                        columns(q0 + ffn_piece("up", j), (pair[j % 2][1],), 0, KD, 2, True, True)
                        if j:
                            down(j - 1)
                    down(NF - 1)
            pe.wait_ge(wr_split, 2)
            for t in range(NT):
                for k in range(KD):
                    ah, al = (x_[:, k, t * P:(t + 1) * P] for x_ in (act_hi, act_lo))
                    mm(bank[4 + t][:, 0:E], ah, wr_hi[:, k, :], start=k == 0, stop=False)
                    mm(bank[4 + t][:, 0:E], ah, wr_lo[:, k, :], start=False, stop=False)
                    ins = mm(bank[4 + t][:, 0:E], al, wr_hi[:, k, :], start=False, stop=k == KD - 1)
                ins.then_inc(logits, 1)
            pe.wait_ge(masks, 1)
            tri = cst[:, C_TRI:C_TRI + P]
            mm(bank[6][:, 0:E], tri, mask[:, 0, :], start=True, stop=True)
            mm(bank[6][:, E:2 * E], ones, mask[:, 0, :], start=True, stop=False)
            mm(bank[6][:, E:2 * E], tri, mask[:, 1, :], start=False, stop=True)
            mm(bank[6][:, 2 * E:3 * E], ones, mask[:, 0, :], start=True, stop=False)
            mm(bank[6][:, 2 * E:3 * E], ones, mask[:, 1, :], start=False, stop=True).then_inc(ranks, 1)

            def gather(r):
                pe.wait_ge(picked, r + 1)
                for k in range(KD):
                    dst = pair[1][k // 4][:, (k % 4) * SLOTS:(k % 4 + 1) * SLOTS]
                    for t in range(NT):
                        cols = slice(k * P, (k + 1) * P)
                        mm(dst, tok_hi[:, t, cols], pick[:, t, :], start=t == 0, stop=False)
                        ins = mm(dst, tok_lo[:, t, cols], pick[:, t, :], start=False, stop=t == NT - 1)
                    if k % 4 == 3:
                        ins.then_inc(gathered, 1)

            def combine(r, t):
                cols = slice(t * P, (t + 1) * P)
                for b in range(2):
                    w = slice(b * 512, (b + 1) * 512)
                    mm(bank[6 + b][:, :], place[:, cols], y_hi[:, w], start=True, stop=False)
                    mm(bank[6 + b][:, :], place[:, cols], y_lo[:, w], start=False, stop=True).then_inc(combined, 1)

            pe.wait_ge(tok_split, 2)
            gather(0)
            pe.wait_ge(routed, 1)
            n_pass = pe.value_load(passes[0:1, 0:1], min_val=1, max_val=2)
            with pe.Fori(0, n_pass) as ps:
                with pe.Fori(0, E) as e:
                    it = ps * E + e
                    before = it * NE_PIECE

                    def gate_up(c, kind):
                        i0 = (0 if c == 0 else 6 * c - 2) + 2 * kind
                        dst = pair[c % 2][kind][:, :]
                        for half in range(2):
                            hi, lo = take(MOE0 + i0 + half, 4, it)
                            for k in range(4):
                                kk = 4 * half + k
                                mm(dst, xe_hi[:, kk, :], hi[:, k, :], start=kk == 0, stop=False)
                                mm(dst, xe_hi[:, kk, :], lo[:, k, :], start=False, stop=False)
                                ins = mm(dst, xe_lo[:, kk, :], hi[:, k, :], start=False, stop=kk == KD - 1)
                            ins.then_inc(used, 1)

                    def turn(c):
                        pe.wait_ge(m_prod, it * CE + (c + 1))
                        if c >= 2:
                            pe.wait_ge(m_alo, it * CE + (c - 1))
                        for b in range(4):
                            ins = nc.tensor.transpose(bank[6 + c % 2][:, b * P:(b + 1) * P],
                                                      prod[c % 2][:, b * P:(b + 1) * P], ident)
                        ins.then_inc(m_tr, 1)

                    def down(c):
                        pe.wait_ge(m_alo, it * CE + (c + 1))
                        for half in range(2):
                            hi, lo = take(MOE0 + (6 * c + 8 if c < CE - 1 else 6 * CE - 2) + half, 2, it)
                            for k in range(2):
                                b = 2 * half + k
                                ah, al = (x_[c % 2][:, b * P:(b + 1) * P] for x_ in (a_hi, a_lo))
                                for o in range(2):
                                    w = slice(o * 512, (o + 1) * 512)
                                    begin, end = c == 0 and b == 0, c == CE - 1 and b == 3
                                    mm(bank[4 + o][:, :], ah, hi[:, k, w], start=begin, stop=False)
                                    mm(bank[4 + o][:, :], ah, lo[:, k, w], start=False, stop=False)
                                    ins = mm(bank[4 + o][:, :], al, hi[:, k, w], start=False, stop=end)
                            ins.then_inc(used, 1)

                    pe.wait_ge(xe_lo_done, it * 2 + 2)
                    gate_up(0, 0)
                    pe.wait_ge(y_lo_done, it * 2 + 2)
                    pe.wait_ge(placed, it + 1)
                    combine(it, 0)
                    gate_up(0, 1)
                    pe.wait_ge(added, it * 4 + 2)
                    combine(it, 1)
                    gate_up(1, 0)
                    pe.wait_ge(added, it * 4 + 4)
                    turn(0)
                    gate_up(1, 1)
                    down(0)
                    pe.wait_ge(gpicked, it + 1)
                    for t in range(NT):
                        ins = nc.tensor.transpose(bank[7][:, t * P:(t + 1) * P], gpick[:, t, :], ident)
                    ins.then_inc(placed_t, 1)
                    for c in range(2, CE):
                        pe.wait_ge(m_prod, it * CE + (c - 1))
                        gate_up(c, 0)
                        if c == 2:
                            pe.wait_ge(placed, it + 2)
                        turn(c - 1)
                        gate_up(c, 1)
                        down(c - 1)
                    turn(CE - 1)
                    gather(it + 1)
                    down(CE - 1)
            rounds = n_pass * E
            pe.wait_ge(y_lo_done, rounds * 2 + 2)
            pe.wait_ge(placed, rounds + 1)
            combine(rounds, 0)
            pe.wait_ge(added, rounds * 4 + 2)
            combine(rounds, 1)


_INS = ['x', 'mem', 'mix_norm_g', 'w_in', 'pool_w', 'pool_scale', 'sconv_w', 'conf_w', 'conf_b', 'conf_ln_g',
        'conf_ln_b', 'group_norm_g', 'w_out', 'mem_norm_g', 'w_mem_kv', 'xattn_norm_g', 'w_q', 'w_o', 'ffn_norm_g',
        'w_gu_dense', 'w_down_dense', 'w_router', 'w_gu_moe', 'w_down_moe', 'final_norm_g']
_OUTS = [((1, S, D), 'float32')]


def constants(np):
    t = np.zeros((P, C_ALL), np.float32)
    p = np.arange(P)
    t[:, C_ID:C_ID + P] = np.eye(P)
    t[:, C_ONE:C_ONE + P] = 1.0
    t[:, C_TRI:C_TRI + P] = p[:, None] < p[None, :]
    t[:, C_IOTA:C_IOTA + P] = p[None, :]
    t[:, C_IOTA8:C_IOTA8 + E] = np.arange(E)
    for b in range(NPOOL):
        for h in range(2):
            count = np.minimum(np.arange(S) + 1, WINDOWS[2 * b + h])
            t[h * P // 2:(h + 1) * P // 2, C_INV + b * S:C_INV + (b + 1) * S] = 1.0 / count
    return t


def kernel(**inputs):
    import numpy as _np
    import concourse.bacc as _bacc
    from concourse import mybir as _mybir
    from concourse.bass_utils import run_bass_kernel_spmd as _run

    nc = _bacc.Bacc("TRN2", target_bir_lowering=False, num_devices=1)
    arrays, args = {}, []
    for name in _INS + ["table"]:
        a = constants(_np) if name == "table" else _np.ascontiguousarray(inputs[name])
        arrays[f"in_{name}_dram"] = a
        args.append(nc.dram_tensor(f"in_{name}_dram", a.shape, _mybir.dt.from_np(a.dtype), kind="ExternalInput").ap())
    for i, (shape, dtype) in enumerate(_OUTS):
        dt = _mybir.dt.from_np(_np.dtype(dtype))
        args.append(nc.dram_tensor(f"out_{i}_dram", shape, dt, kind="ExternalOutput").ap())
    trunk(nc, *args)
    r = _run(nc, [arrays], core_ids=[0])
    got = tuple(r.results[0][f"out_{i}_dram"] for i in range(len(_OUTS)))
    return got[0]
```

```python
from contextlib import ExitStack

import concourse.bass as bass
from concourse import mybir

ALU = mybir.AluOpType
ACT = mybir.ActivationFunctionType
AX = mybir.AxisListType
F32 = mybir.dt.float32
F32R = mybir.dt.float32r
I32 = mybir.dt.int32
U32 = mybir.dt.uint32

P = 128
D = 1024
S = 256
NT = S // P
KD = D // P
EPS = 1e-6
NPOOL, NSC, NCONF = 2, 3, 3
NZ = NPOOL + 3 * NSC + 2 * NCONF
TAPS, SCTAPS = 31, 3
WINDOWS = (2, 4, 8, 16)
HEADS = 4
FF = 2816
NF = FF // 256
E = 8
FE = 3584
CE = FE // 512
SLOTS = 128

PIECE = 2048
RAW = 7
SPLIT = 3
AHEAD = SPLIT - 1
AHEAD_E = SPLIT

C_ID, C_ONE, C_TRI, C_IOTA, C_INV = 0, 128, 256, 384, 512
C_IOTA8 = C_INV + 2 * S
C_MEAN = C_IOTA8 + 8
C_ALL = C_MEAN + 128

ROWS = {}
_at = 0
for _name, _n in (("pool_scale", 2 * NPOOL), ("sconv_w", 2 * SCTAPS * NSC), ("conf_b", 2 * NCONF),
                  ("conf_ln_g", 2 * NCONF), ("conf_ln_b", 2 * NCONF), ("group_norm_g", 2 * KD)):
    ROWS[_name] = _at
    _at += _n
NROW = _at
NCW = TAPS * NCONF

WIN_CHUNKS = ((13, 4), (9, 4), (0, 4), (5, 4), (4, 1))
N_WIN, N_KV, N_SQ, N_FFN = 9, 8, 4, 3 * NF


def layer_base(layer):
    q = n = 0
    out = {}
    for m in range(layer + 1):
        for name, pieces, chunks in (("win", N_WIN, len(WIN_CHUNKS)), ("kv", N_KV * (m == 0), 4 * (m == 0)),
                                     ("wout", N_SQ, 4), ("wq", N_SQ, 2), ("wo", N_SQ, 2),
                                     ("ffn", N_FFN * (m == 0), 0)):
            if m == layer:
                out[name] = (q, n)
            q += pieces
            n += chunks
    out["end"] = (q, n)
    return out


BASE = (layer_base(0), layer_base(1))
MOE0 = BASE[1]["end"][0]
NE_PIECE = 6 * CE

CONF_DVE = ("conv", "centred", "scaled0", "scaled1", "scaled2", "lo_conf0", "lo_conf1", "lo_conf2")
CONF_ACT = ("conf_sq", "conf_sd", "hi_conf0", "hi_conf1", "hi_conf2", "rms_sq", "rms_sd")
MIX_DVE = (("prod", "sconv_y", "pool_y", "y_sconv", "y_pool", "lo_pool", "lo_sconv") + CONF_DVE,
           ("prod", "pool_y", "sconv_y", "y_pool", "y_sconv", "lo_pool", "lo_sconv") + CONF_DVE)
MIX_ACT = (("sconv_sq", "sconv_sd", "pool_sq", "pool_sd", "hi_pool", "hi_sconv") + CONF_ACT,
           ("pool_sq", "pool_sd", "sconv_sq", "sconv_sd", "hi_pool", "hi_sconv") + CONF_ACT)
MIX_PE = (("pool", "sconv_ssq", "pool_ssq", "mean", "var", "rms_ssq"),
          ("pool", "pool_ssq", "sconv_ssq", "mean", "var", "rms_ssq"))
CONV_PE = ((), ((2, 0), (1, 19)))
CONV_FULL, CONV_PART = 2, 1


def step(steps, name, layer):
    return sum(len(steps[m]) for m in range(layer)) + steps[layer].index(name) + 1


def ffn_piece(kind, j):
    if kind == "down":
        return 3 * (j + 1) + 1 if j < NF - 1 else 3 * NF - 1
    return (0 if j == 0 else 3 * j - 1) + (kind == "up")


def trunk(nc, x, mem, mix_norm_g, w_in, pool_w, pool_scale, sconv_w, conf_w, conf_b, conf_ln_g,
          conf_ln_b, group_norm_g, w_out, mem_norm_g, w_mem_kv, xattn_norm_g, w_q, w_o, ffn_norm_g,
          w_gu_dense, w_down_dense, w_router, w_gu_moe, w_down_moe, final_norm_g, table, out):
    with ExitStack() as ctx:
        def sb(name, shape, dt=F32, scope=ctx):
            return scope.enter_context(nc.sbuf_tensor(name, shape, dt))

        def sem(name):
            return ctx.enter_context(nc.semaphore(name))

        raw = [sb(f"raw{i}", [P, PIECE]) for i in range(RAW)]
        w_hi = [sb(f"w_hi{i}", [P, PIECE], F32R) for i in range(SPLIT)]
        w_lo = [sb(f"w_lo{i}", [P, PIECE], F32R) for i in range(SPLIT)]
        res = sb("res", [P, NT, D])
        xn = sb("xn", [P, NT, D])
        gain = sb("gain", [P, D])
        act_hi = sb("act_hi", [P, KD, S], F32R)
        act_lo = sb("act_lo", [P, KD, S], F32R)
        cst = sb("cst", [P, C_ALL])
        rows = sb("rows", [P, 3, P])
        par = sb("par", [P, NROW + 2 * NCW])
        pool_bd = sb("pool_bd", [P, 2 * NPOOL, P])
        wr = sb("wr", [P, KD, E])
        small = sb("small", [P, 64])
        diag_more = sb("diag_more", [P, 4, P])
        group_sd, group_rstd = small[:, 36:38], small[:, 38:40]
        ident, ones = cst[:, C_ID:C_ID + P], cst[:, C_ONE:C_ONE + P]
        part = small[:, 32:36].rearrange("p (t c) -> p t c", t=NT)
        ss, rstd = small[:, 0:2], small[:, 2:4]
        sd = small[:, 4:6]
        eps_col = small[:, 6:7]
        top_neg, top_sum, top_inv = small[:, 8:16], small[:, 16:24], small[:, 24:32]

        dense = ctx.enter_context(ExitStack())
        kT = sb("kT", [P, KD, S], scope=dense)
        v = sb("v", [P, NT, D], scope=dense)
        hpad = sb("hpad", [P, NCONF, TAPS - 1 + S], scope=dense)
        upad = sb("upad", [P, NPOOL, 16 + S], scope=dense)
        win2 = sb("win2", [P, NPOOL, 16 + S], scope=dense)
        win4 = sb("win4", [P, NPOOL, 16 + S], scope=dense)
        win8 = sb("win8", [P, 16 + S], scope=dense)
        win16 = sb("win16", [P, 16 + S], scope=dense)
        spad = sb("spad", [P, NSC, SCTAPS - 1 + S], scope=dense)
        stat = sb("stat", [P, 8, S], scope=dense)
        mixer = dense.enter_context(ExitStack())
        z = sb("z", [P, NZ, S], scope=mixer)
        mixer.close()
        ffn = dense.enter_context(ExitStack())
        f_sil = [sb(f"f_sil{i}", [P, 512], scope=ffn) for i in range(2)]
        f_a = [sb(f"f_a{i}", [P, 512], scope=ffn) for i in range(2)]
        f_hi = [sb(f"f_hi{i}", [P, 512], F32R, scope=ffn) for i in range(2)]
        f_lo = [sb(f"f_lo{i}", [P, 512], F32R, scope=ffn) for i in range(2)]
        ffn.close()
        dense.close()
        moe = ctx.enter_context(ExitStack())
        xe_hi = sb("xe_hi", [P, KD, SLOTS], F32R, scope=moe)
        xe_lo = sb("xe_lo", [P, KD, SLOTS], F32R, scope=moe)
        y_hi = sb("y_hi", [P, D], F32R, scope=moe)
        y_lo = sb("y_lo", [P, D], F32R, scope=moe)
        sil = [sb(f"sil{i}", [P, 512], scope=moe) for i in range(2)]
        prod = [sb(f"prod{i}", [P, 512], scope=moe) for i in range(2)]
        a_hi = [sb(f"a_hi{i}", [P, 512], F32R, scope=moe) for i in range(2)]
        a_lo = [sb(f"a_lo{i}", [P, 512], F32R, scope=moe) for i in range(2)]
        wr_hi = sb("wr_hi", [P, KD, E], F32R, scope=moe)
        wr_lo = sb("wr_lo", [P, KD, E], F32R, scope=moe)
        pick = sb("pick", [P, NT, SLOTS], F32R, scope=moe)
        gpick = sb("gpick", [P, NT, SLOTS], scope=moe)
        place = sb("place", [P, S], F32R, scope=moe)
        rank = sb("rank", [P, NT, 2 * E + 1], scope=moe)
        gate = sb("gate", [P, NT, 2 * E + 1], scope=moe)
        best = sb("best", [P, NT, E], scope=moe)
        idx8 = sb("idx8", [P, NT, E], U32, scope=moe)
        idx = sb("idx", [P, NT, E], scope=moe)
        hot = sb("hot", [P, 2, NT, E], scope=moe)
        mask = sb("mask", [P, NT, E], scope=moe)
        slot1 = sb("slot1", [P, NT, E], scope=moe)
        diff = sb("diff", [P, NT, 1], scope=moe)
        ex = sb("ex", [P, NT, 1], scope=moe)
        gw = sb("gw", [P, 2, NT, 1], scope=moe)
        logit = sb("logit", [E, S], scope=moe)
        tok_hi = sb("tok_hi", [P, NT, D], F32R, scope=moe)
        tok_lo = sb("tok_lo", [P, NT, D], F32R, scope=moe)
        cnt = sb("cnt", [P, 2], scope=moe)
        rcol = sb("rcol", [P, NT, 1], scope=moe)
        gcol = sb("gcol", [P, NT, 1], scope=moe)
        gslot = sb("gslot", [P, 1], scope=moe)
        passes = sb("passes", [P, 1], I32, scope=moe)
        zero = sb("zero", [P, 512], scope=moe)

        bank = [ctx.enter_context(nc.psum_tensor(f"bank{i}", [P, 512], F32)) for i in range(8)]
        pair = ((bank[0], bank[1]), (bank[2], bank[3]))

        scr = xn[:, :, :].rearrange("p t d -> p (t d)").rearrange("p (b s) -> p b s", s=S)
        z_sq = scr
        halves = [t[:, b, h * P:(h + 1) * P] for t, bs in ((stat, (5, 6, 7, 0, 1, 2)), (z, (14, 15, 16)), (scr, (5, 6, 7)))
                  for b in bs for h in range(2)]
        diag = [diag_more[:, i, :] for i in range(4)] + [rows[:, i, :] for i in range(3)] + halves
        DIAG_WIN = len(diag)
        diag += [t[:, :, :].rearrange("p b s -> p (b s)")[:, i * P:(i + 1) * P] for t in (win2, win4, upad)
                 for i in range(4)]
        conv_taps_pe = [[(b, k) for b, k0 in CONV_PE[m] for k in range(k0, TAPS)] for m in range(2)]

        raw_in = [sem(f"raw_in{i}") for i in range(RAW)]
        hi_done = sem("hi_done")
        lo_done = sem("lo_done")
        used = sem("used")
        pair_free = [sem(f"pair_free{i}") for i in range(2)]
        s_x = [sem(f"x_in{t}") for t in range(NT)]
        s_mem, s_cst, s_rows, s_wr, s_pw = (sem(n) for n in ("mem_in", "cst_in", "rows_in", "wr_in", "poolw_in"))
        conf_silu = sem("conf_silu")
        ffn_half = sem("ffn_first_half")
        group_a, out_half = sem("out_pool_sconv"), sem("out_first_half")
        diags, conv_pe, conv_act = sem("diags"), sem("conv_pe"), sem("conv_act")
        squared, res_added = sem("squared"), sem("res_added")
        s_gain0, s_gain = sem("first_gain_in"), sem("gain_in")
        eps_set = sem("eps_set")
        pads = sem("pads_zeroed")
        bd_zero = sem("pool_bd_zeroed")
        par_t = sem("par_transposed")
        par_c = sem("par_copied")
        norm_ss, norm_sd, norm_x = sem("norm_ss"), sem("norm_sd"), sem("norm_x")
        norm_t, norm_hi, norm_lo = sem("norm_t"), sem("norm_hi"), sem("norm_lo")
        mix_dve, mix_act, mix_pe, mix_pool = sem("mix_dve"), sem("mix_act"), sem("mix_pe"), sem("mix_pool")
        scores, top, probs, normed = sem("scores"), sem("top"), sem("probs"), sem("normed")
        pt, pt_even, pt_odd = sem("pt"), sem("pt_even_copied"), sem("pt_odd_copied")
        attn_o, o_hi, o_lo = sem("attn_o"), sem("o_hi"), sem("o_lo")
        f_silu, f_prod, f_ahi, f_alo = sem("f_silu"), sem("f_prod"), sem("f_ahi"), sem("f_alo")
        chain = sem("dve_chain")
        loop_chain = sem("dve_loop_chain")
        pchain = sem("pool_chain")
        wr_split = sem("wr_split")
        logits_t, logits_copied = sem("logits_t"), sem("logits_copied")
        logits, masks, ranks, routed = sem("logits"), sem("masks"), sem("ranks"), sem("routed")
        margins, r_exp = sem("router_margins"), sem("router_exp")
        tok_split = sem("tok_split")
        picked, gpicked = sem("picked"), sem("gpicked")
        gathered, xe_hi_done, xe_lo_done = sem("gathered"), sem("xe_hi_done"), sem("xe_lo_done")
        placed_t, placed = sem("placed_t"), sem("placed")
        m_sil, m_prod, m_tr, m_ahi, m_alo = sem("m_sil"), sem("m_prod"), sem("m_tr"), sem("m_ahi"), sem("m_alo")
        y_hi_done, y_lo_done = sem("y_hi_done"), sem("y_lo_done")
        combined, added = sem("combined"), sem("added")
        s_out = sem("out_stored")

        def kn(w, rows0, nk, c0, n):
            return w[rows0:rows0 + nk * P, c0:c0 + n].rearrange("(k p) n -> p k n", p=P)

        def dense_stream():
            for layer in range(2):
                for b0, nb in WIN_CHUNKS[:-1]:
                    for half in range(2):
                        yield kn(w_in[layer], half * 512, 4, b0 * P, 512)
                yield kn(w_in[layer], 0, KD, WIN_CHUNKS[-1][0] * P, P)
                if layer == 0:
                    for c in range(4):
                        for half in range(2):
                            yield kn(w_mem_kv, half * 512, 4, c * 512, 512)
                for i in range(4):
                    yield kn(w_out[layer], i * 256, 2, 0, D)
                for w in (w_q[layer], w_o[layer]):
                    for c in range(2):
                        for half in range(2):
                            yield kn(w, half * 512, 4, c * 512, 512)
                if layer == 0:
                    down = [kn(w_down_dense[0], j * 256, 2, 0, D) for j in range(NF)]
                    for j in range(NF):
                        yield kn(w_gu_dense[0], 0, KD, j * 256, 256)
                        yield kn(w_gu_dense[0], 0, KD, FF + j * 256, 256)
                        if j:
                            yield down[j - 1]
                    yield down[NF - 1]

        def expert_pieces():
            out = []
            for c in range(CE):
                out += [("gate", c, 0), ("gate", c, 1), ("up", c, 0), ("up", c, 1)]
                if c:
                    out += [("down", c - 1, 0), ("down", c - 1, 1)]
            return out + [("down", CE - 1, 0), ("down", CE - 1, 1)]

        EP = expert_pieces()

        def expert_src(e, i):
            kind, c, half = EP[i]
            if kind == "down":
                w = w_down_moe[0, e, (c * 4 + half * 2) * P:(c * 4 + half * 2 + 2) * P, :]
                return w.rearrange("(k p) n -> p k n", p=P)
            c0 = c * 512 + (FE if kind == "up" else 0)
            return w_gu_moe[0, e, half * 512:half * 512 + 512, c0:c0 + 512].rearrange("(k p) n -> p k n", p=P)

        DENSE = list(dense_stream())
        SIZES = [s.shape[1] * s.shape[2] for s in DENSE]

        def load(sp, q, src, raw_free):
            nk, n = src.shape[1], src.shape[2]
            if raw_free is not None:
                sp.wait_ge(lo_done, raw_free)
            dst = raw[q % RAW][:, 0:nk * n].rearrange("p (k n) -> p k n", k=nk)
            sp.dma_start(dst, src).then_inc(raw_in[q % RAW], 16)

        def split_hi(act, q, n=PIECE, it=None):
            landed, left = 16 * (q // RAW + 1), q - SPLIT + 1
            if it is None:
                act.wait_ge(raw_in[q % RAW], landed)
                if left > 0:
                    act.wait_ge(used, left)
            else:
                act.wait_ge(raw_in[q % RAW], it * (16 * NE_PIECE // RAW) + landed)
                act.wait_ge(used, it * NE_PIECE + left)
            nc.scalar.activation(w_hi[q % SPLIT][:, 0:n], raw[q % RAW][:, 0:n], ACT.Copy).then_inc(hi_done, 1)

        def split_lo(dve, q, n=PIECE, it=None):
            dve.wait_ge(hi_done, q + 1 if it is None else it * NE_PIECE + (q + 1))
            nc.vector.tensor_tensor(w_lo[q % SPLIT][:, 0:n], raw[q % RAW][:, 0:n],
                                    w_hi[q % SPLIT][:, 0:n].bitcast(F32), ALU.subtract).then_inc(lo_done, 1)

        block = ctx.enter_context(nc.Block())

        @block.sync
        def _(sp):
            for t in range(NT):
                sp.dma_start(res[:, t, :], x[0, t * P:(t + 1) * P, :]).then_inc(s_x[t], 16)
            for q, src in enumerate(DENSE):
                if q == 4:
                    sp.dma_start(v[:, :, :], mem[0].rearrange("(t p) d -> p t d", p=P)).then_inc(s_mem, 16)
                load(sp, q, src, q - RAW + 1 if q >= RAW else None)

            def expert_round(pass_pieces, e):
                for i in range(AHEAD_E, NE_PIECE):
                    load_expert(e, i, pass_pieces)
                nxt = (e + 1) % E
                for i in range(AHEAD_E):
                    load_expert(nxt, NE_PIECE + i, pass_pieces)

            def load_expert(e, i, before):
                sp.wait_ge(lo_done, before + (MOE0 + i - RAW + 1))
                q = MOE0 + i
                src = expert_src(e, i % NE_PIECE)
                dst = raw[q % RAW][:, :].rearrange("p (k n) -> p k n", k=src.shape[1])
                sp.dma_start(dst, src).then_inc(raw_in[q % RAW], 16)

            for i in range(AHEAD_E):
                load_expert(0, i, 0)
            with sp.Fori(0, E) as e:
                expert_round(e * NE_PIECE, e)
            sp.wait_ge(routed, 1)
            n_pass = sp.value_load(passes[0:1, 0:1], min_val=1, max_val=2)
            with sp.If(n_pass > 1):
                with sp.Fori(0, E) as e:
                    expert_round((e + E) * NE_PIECE, e)
            for t in range(NT):
                sp.wait_ge(norm_x, 4 * 7 + 2 * (t + 1))
                sp.dma_start(out[0, t * P:(t + 1) * P, :], xn[:, t, :]).then_inc(s_out, 16)
            sp.wait_ge(s_out, 16 * NT)

        @block.gpsimd
        def _(pool):
            gains = (mix_norm_g[0:1, :], mem_norm_g.rearrange("(a d) -> a d", a=1), xattn_norm_g[0:1, :],
                     ffn_norm_g[0:1, :], mix_norm_g[1:2, :], xattn_norm_g[1:2, :], ffn_norm_g[1:2, :],
                     final_norm_g.rearrange("(a d) -> a d", a=1))

            def load_gain(n):
                pool.wait_ge(norm_x, 4 * n)
                pool.dma_start(gain[:, :], gains[n].partition_broadcast(P)
                               if len(gains[n].shape) == 1 else gains[n].broadcast_to([P, D])).then_inc(s_gain, 16)

            nc.gpsimd.memset(pool_bd[:, :, :], 0.0).then_inc(bd_zero, 1)
            for name, src in (("pool_scale", pool_scale), ("conf_b", conf_b), ("conf_ln_g", conf_ln_g),
                              ("conf_ln_b", conf_ln_b), ("group_norm_g", group_norm_g)):
                src = src.rearrange("l (b p) -> (l b) p", p=P)
                pool.dma_start(rows[ROWS[name]:ROWS[name] + src.shape[0], 0, :], src).then_inc(s_rows, 16)
            src = sconv_w.rearrange("l k (b p) -> (l k b) p", p=P)
            pool.dma_start(rows[ROWS["sconv_w"]:ROWS["sconv_w"] + src.shape[0], 0, :], src).then_inc(s_rows, 16)
            for layer in range(2):
                src = conf_w[layer].rearrange("k (b p) -> (k b) p", p=P)
                pool.dma_start(rows[0:NCW, 1 + layer, :], src).then_inc(s_rows, 16)
            for t in (hpad, upad, spad):
                nc.gpsimd.memset(t[:, :, :], 0.0)
            nc.gpsimd.memset(win2[:, :, :], 0.0)
            nc.gpsimd.memset(win4[:, :, :], 0.0)
            nc.gpsimd.memset(win8[:, :], 0.0)
            nc.gpsimd.memset(win16[:, :], 0.0).then_inc(pads, 1)
            load_gain(1)
            pool.wait_ge(bd_zero, 1)
            for layer in range(2):
                for g in range(4):
                    h = P // 2 * (g % 2)
                    pool.dma_start(pool_bd[h:h + P // 2, layer * NPOOL + g // 2, h:h + P // 2],
                                   pool_w[layer, g]).then_inc(s_pw, 16)
            pool.dma_start(wr[:, :, :], w_router[0].rearrange("(k p) e -> p k e", p=P)).then_inc(s_wr, 16)
            pool.wait_ge(pads, 1)
            steps = [0]

            def link(ins):
                steps[0] += 1
                ins.then_inc(pchain, 1)
                pool.wait_ge(pchain, steps[0])

            pool.wait_ge(s_cst, 16)
            for layer in range(2):
                if layer:
                    load_gain(5)
                n0 = BASE[layer]["win"][1]
                n = n0 + 2
                pool.wait_ge(pair_free[n % 2], n // 2 + 1)
                H = 16
                link(nc.gpsimd.tensor_tensor(win2[:, :, H:], upad[:, :, H:], upad[:, :, H - 1:H - 1 + S], ALU.add))
                link(nc.gpsimd.tensor_tensor(win4[:, :, H:], win2[:, :, H:], win2[:, :, H - 2:H - 2 + S], ALU.add))
                link(nc.gpsimd.tensor_tensor(win8[:, H:], win4[:, 1, H:], win4[:, 1, H - 4:H - 4 + S], ALU.add))
                link(nc.gpsimd.tensor_tensor(win16[:, H:], win8[:, H:], win8[:, H - 8:H - 8 + S], ALU.add))
                inv = cst[:, C_INV:C_INV + 2 * S].rearrange("p (b s) -> p b s", b=2)
                h = P // 2
                for b, lo_w, hi_w in ((0, win2[0:h, 0, H:], win4[h:P, 0, H:]), (1, win8[0:h, H:], win16[h:P, H:])):
                    nc.gpsimd.tensor_tensor(z[0:h, b, :], lo_w, inv[0:h, b, :], ALU.mult)
                    link(nc.gpsimd.tensor_tensor(z[h:P, b, :], hi_w, inv[h:P, b, :], ALU.mult))
                nc.gpsimd.tensor_tensor(z[:, 0:NPOOL, :], z[:, 0:NPOOL, :], upad[:, :, H:],
                                        ALU.subtract).then_inc(mix_pool, 1)
                if layer == 0:
                    load_gain(2)
                    load_gain(3)
                    load_gain(4)
                else:
                    load_gain(6)
                    load_gain(7)

        @block.scalar
        def _(act):
            act.dma_start(cst[:, :], table).then_inc(s_cst, 16)
            act.dma_start(gain[:, :], mix_norm_g[0:1, :].broadcast_to([P, D])).then_inc(s_gain0, 16)

            unread = iter(range(40, 64))

            def preload(function):
                c = next(unread)
                nc.scalar.activation(small[:, c:c + 1], eps_col, function)

            qn = [0]

            def hi_upto(q):
                while qn[0] <= q:
                    split_hi(act, qn[0], SIZES[qn[0]] if qn[0] < MOE0 else PIECE)
                    qn[0] += 1

            def norm(n, src=res, landed=None, last_adds=None):
                preload(ACT.Sqrt)
                for c in range(2):
                    if last_adds is not None:
                        act.wait_ge(added, last_adds + (c + 1))
                    elif landed is None:
                        act.wait_ge(res_added, 2 * (n - 2) + c + 1)
                    elif c == 0:
                        act.wait_ge(landed, 16)
                    cols = slice(c * 512, (c + 1) * 512)
                    nc.scalar.activation(xn[:, 0, cols], src[:, 0, cols], ACT.Square,
                                         accum_out=part[:, 0, c:c + 1]).then_inc(squared, 1)
                act.wait_ge(norm_ss, n + 1)
                nc.scalar.activation(sd, ss, ACT.Sqrt, scale=1.0 / D, bias=eps_col).then_inc(norm_sd, 1)

            def norm_split(n):
                for g in range(2):
                    for t in range(NT):
                        act.wait_ge(norm_t, 4 * n + 2 * g + t + 1)
                        nc.scalar.activation(act_hi[:, 4 * g:4 * g + 4, t * P:(t + 1) * P],
                                             bank[4 + 2 * g + t][:, :].rearrange("p (k s) -> p k s", k=4),
                                             ACT.Copy).then_inc(norm_hi, 1)

            act.wait_ge(eps_set, 1)
            norm(0, landed=s_x[0])
            hi_upto(0)
            for layer in range(2):
                q0, n0 = BASE[layer]["win"]
                norm_i = 0 if layer == 0 else 4
                if layer:
                    norm(4)
                norm_split(norm_i)
                taps_made = [0]

                def diagonals(n):
                    for i in range(taps_made[0], min(taps_made[0] + n, len(conv_taps_pe[layer]))):
                        b, k = conv_taps_pe[layer][i]
                        if i == 0:
                            act.wait_ge(mix_dve, step(MIX_DVE, "prod", layer))
                        if i == DIAG_WIN:
                            act.wait_ge(mix_pool, layer + 1)
                        col = NROW + layer * NCW + k * NCONF + b
                        nc.scalar.activation(diag[i], ident, ACT.Copy, scale=par[:, col:col + 1]).then_inc(diags, 1)
                        taps_made[0] += 1

                conf = z[:, 11:14, :]

                def d(name):
                    act.wait_ge(mix_dve, step(MIX_DVE, name, layer))

                def pe_(name):
                    act.wait_ge(mix_pe, step(MIX_PE, name, layer))

                def sconv_squares():
                    d("sconv_y")
                    nc.scalar.activation(z_sq[:, 2:5, :], z[:, 2:5, :], ACT.Square).then_inc(mix_act, 1)

                def sconv_root():
                    pe_("sconv_ssq")
                    nc.scalar.activation(stat[:, 4, :], bank[4][:, 0:S], ACT.Sqrt, scale=1.0 / 384,
                                         bias=eps_col).then_inc(mix_act, 1)

                def pool_squares():
                    d("pool_y")
                    nc.scalar.activation(z_sq[:, 0:2, :], z[:, 0:2, :], ACT.Square).then_inc(mix_act, 1)

                def group_hi(name, b0, b1):
                    d("y_" + name)
                    nc.scalar.activation(act_hi[:, b0:b1, :], z[:, b0:b1, :], ACT.Copy).then_inc(mix_act, 1)

                def pool_root():
                    pe_("pool_ssq")
                    nc.scalar.activation(stat[:, 3, :], bank[5][:, 0:S], ACT.Sqrt, scale=1.0 / 256,
                                         bias=eps_col).then_inc(mix_act, 1)

                for c, (b0, nb) in enumerate(WIN_CHUNKS):
                    n = n0 + c
                    last = q0 + (2 * c + 1 if c < 4 else 8)
                    hi_upto(last + AHEAD)
                    if c == 0:
                        preload(ACT.Sigmoid)
                    if layer and c == 4:
                        pool_squares()
                    act.wait_ge(used, last + 1)
                    lo_bank, hi_bank = pair[n % 2]
                    if c == 0:
                        nc.scalar.activation(z[:, b0, :], lo_bank[:, 0:S], ACT.Copy)
                        nc.scalar.activation(z[:, b0 + 1, :], lo_bank[:, S:2 * S], ACT.Sigmoid)
                        nc.scalar.activation(z[:, b0 + 2:b0 + 4, :], hi_bank[:, :].rearrange("p (b s) -> p b s", s=S),
                                             ACT.Sigmoid).then_inc(pair_free[n % 2], 1)
                    elif c == 2:
                        nc.scalar.activation(upad[:, :, 16:], lo_bank[:, :].rearrange("p (b s) -> p b s", s=S), ACT.Copy)
                        nc.scalar.activation(z[:, b0 + 2:b0 + 4, :], hi_bank[:, :].rearrange("p (b s) -> p b s", s=S),
                                             ACT.Copy).then_inc(pair_free[n % 2], 1)
                    elif nb == 4:
                        nc.scalar.activation(z[:, b0:b0 + 2, :], lo_bank[:, :].rearrange("p (b s) -> p b s", s=S),
                                             ACT.Copy)
                        nc.scalar.activation(z[:, b0 + 2:b0 + 4, :], hi_bank[:, :].rearrange("p (b s) -> p b s", s=S),
                                             ACT.Copy).then_inc(pair_free[n % 2], 1)
                    else:
                        nc.scalar.activation(z[:, b0, :], lo_bank[:, 0:S], ACT.Copy).then_inc(pair_free[n % 2], 1)
                    if c == 0:
                        act.wait_ge(pads, 1)
                    if c >= 1:
                        diagonals(9 if c < 4 else TAPS * NCONF)
                    if layer == 0 and c == 0:
                        act.wait_ge(norm_t, 4)
                        norm(1, v, s_mem)
                if layer == 0:
                    norm_split(1)
                    q0, n0 = BASE[0]["kv"]
                    for c in range(4):
                        n = n0 + c
                        hi_upto(q0 + 2 * c + 1 + AHEAD)
                        if c == 2:
                            sconv_root()
                            pool_squares()
                        act.wait_ge(used, q0 + 2 * c + 2)
                        if c == 3:
                            group_hi("pool", 0, 2)
                        if c < 2:
                            for i in range(2):
                                ins = nc.scalar.activation(kT[:, 4 * c + 2 * i:4 * c + 2 * i + 2, :],
                                                           pair[n % 2][i][:, :].rearrange("p (b s) -> p b s", s=S),
                                                           ACT.Copy)
                        else:
                            for t in range(NT):
                                ins = nc.scalar.activation(v[:, t, (c - 2) * 512:(c - 1) * 512], pair[n % 2][t][:, :],
                                                           ACT.Copy)
                        ins.then_inc(pair_free[n % 2], 1)
                        if c == 0:
                            sconv_squares()
                            preload(ACT.Sqrt)
                        elif c == 2:
                            pool_root()
                else:
                    pool_root()
                    hi_upto(BASE[layer]["wout"][0] + SPLIT - 1)
                    sconv_squares()
                    sconv_root()
                    group_hi("pool", 0, 2)
                q0, n0 = BASE[layer]["wout"]
                group_hi("sconv", 2, 5)
                if CONV_PE[layer]:
                    b = CONV_FULL
                    cb = ROWS["conf_b"] + layer * NCONF + b
                    act.wait_ge(conv_pe, 1)
                    nc.scalar.activation(z[:, 11 + b, :], bank[7][:, 0:S], ACT.Identity,
                                         bias=par[:, cb:cb + 1]).then_inc(conv_act, 1)
                hi_upto(q0 + 3)
                preload(ACT.Sqrt)
                d("centred")
                nc.scalar.activation(z_sq[:, 5:8, :], conf, ACT.Square).then_inc(mix_act, 1)
                pe_("var")
                nc.scalar.activation(stat[:, 1, :], bank[5][:, 0:S], ACT.Sqrt, scale=1.0 / 384,
                                     bias=eps_col).then_inc(mix_act, 1)
                preload(ACT.Silu)

                def conf_hi(b):
                    gg = ROWS["group_norm_g"] + layer * KD + 5 + b
                    act.wait_ge(conf_silu, layer * NCONF + b + 1)
                    nc.scalar.activation(act_hi[:, 5 + b, :], z[:, 11 + b, :], ACT.Copy,
                                         scale=par[:, gg:gg + 1]).then_inc(mix_act, 1)

                for b in range(NCONF):
                    if b == NCONF - 1:
                        conf_hi(0)
                    g, bb = (par[:, ROWS[name] + layer * NCONF + b:ROWS[name] + layer * NCONF + b + 1]
                             for name in ("conf_ln_g", "conf_ln_b"))
                    d(f"scaled{b}")
                    nc.scalar.activation(z[:, 11 + b, :], z[:, 11 + b, :], ACT.Silu, scale=g,
                                         bias=bb).then_inc(conf_silu, 1)
                for b in range(1, NCONF):
                    conf_hi(b)
                nc.scalar.activation(z_sq[:, 5:8, :], conf, ACT.Square).then_inc(mix_act, 1)
                hi_upto(q0 + N_SQ - 1 + AHEAD)
                preload(ACT.Sqrt)
                pe_("rms_ssq")
                nc.scalar.activation(group_sd, bank[4][:, 0:NT], ACT.Sqrt, scale=1.0 / 384,
                                     bias=eps_col).then_inc(mix_act, 1)
                norm_i += 2 if layer == 0 else 1
                norm(norm_i)
                norm_split(norm_i)
                q0, n0 = BASE[layer]["wq"]
                for c in range(2):
                    n = n0 + c
                    hi_upto(q0 + 2 * c + 1 + AHEAD)
                    act.wait_ge(used, q0 + 2 * c + 2)
                    for i in range(2):
                        ins = nc.scalar.activation(scr[:, 4 * c + 2 * i:4 * c + 2 * i + 2, :],
                                                   pair[n % 2][i][:, :].rearrange("p (b s) -> p b s", s=S), ACT.Copy)
                    ins.then_inc(pair_free[n % 2], 1)
                preload(ACT.Exp)
                for h in range(HEADS):
                    act.wait_ge(top, layer * HEADS + h + 1)
                    for t in range(NT):
                        i = 2 * h + t
                        ins = nc.scalar.activation(z[:, i, :], bank[4 + h][:, t * S:(t + 1) * S], ACT.Exp,
                                                   scale=1.0 / 16, bias=top_neg[:, i:i + 1],
                                                   accum_out=top_sum[:, i:i + 1])
                    ins.then_inc(probs, 1)
                for h in range(0, HEADS, 2):
                    act.wait_ge(pt, layer * HEADS + h + 1)
                    nc.scalar.activation(z[:, 8 + 2 * h:10 + 2 * h, :],
                                         bank[4 + h][:, :].rearrange("p (b s) -> p b s", s=S),
                                         ACT.Copy).then_inc(pt_even, 1)
                for h in range(HEADS):
                    act.wait_ge(attn_o, layer * HEADS + h + 1)
                    nc.scalar.activation(act_hi[:, 2 * h:2 * h + 2, :],
                                         bank[4 + h][:, :].rearrange("p (b s) -> p b s", s=S),
                                         ACT.Copy).then_inc(o_hi, 1)
                q0, n0 = BASE[layer]["wo"]
                hi_upto(q0 + N_SQ - 1 + AHEAD)
                norm_i += 1
                norm(norm_i)
                norm_split(norm_i)
                if layer == 0:
                    q0, n0 = BASE[0]["ffn"]
                    preload(ACT.Silu)
                    for j in range(NF):
                        g = q0 + ffn_piece("gate", j)
                        hi_upto(g + AHEAD)
                        act.wait_ge(used, g + 1)
                        if j >= 2:
                            act.wait_ge(f_prod, j - 1)
                        nc.scalar.activation(f_sil[j % 2][:, :], pair[j % 2][0][:, :], ACT.Silu).then_inc(f_silu, 1)
                        hi_upto(g + 1 + AHEAD)
                        act.wait_ge(f_prod, j + 1)
                        if j >= 2:
                            act.wait_ge(used, q0 + ffn_piece("down", j - 2) + 1)
                        nc.scalar.activation(f_hi[j % 2][:, :], f_a[j % 2][:, :], ACT.Copy).then_inc(f_ahi, 1)
                    hi_upto(q0 + N_FFN - 1 + AHEAD)
            act.wait_ge(s_wr, 16)
            nc.scalar.activation(wr_hi[:, :, :], wr[:, :, :], ACT.Copy).then_inc(wr_split, 1)
            hi_upto(MOE0 + AHEAD_E - 1)
            nc.scalar.activation(tok_hi[:, :, :], xn[:, :, :], ACT.Copy).then_inc(tok_split, 1)
            preload(ACT.Exp)
            act.wait_ge(margins, 1)
            nc.scalar.activation(ex[:, :, :], diff[:, :, :], ACT.Exp).then_inc(r_exp, 1)
            preload(ACT.Silu)

            def gather_hi(r):
                for b in range(2):
                    act.wait_ge(gathered, r * 2 + (b + 1))
                    nc.scalar.activation(xe_hi[:, 4 * b:4 * b + 4, :], pair[1][b][:, :].rearrange("p (k s) -> p k s", k=4),
                                         ACT.Copy).then_inc(xe_hi_done, 1)

            gather_hi(0)
            act.wait_ge(routed, 1)
            n_pass = act.value_load(passes[0:1, 0:1], min_val=1, max_val=2)
            with act.Fori(0, n_pass) as ps:
                with act.Fori(0, E) as e:
                    it = ps * E + e
                    before = it * NE_PIECE

                    def hi(i0, i1):
                        for i in range(i0, i1):
                            split_hi(act, MOE0 + i, it=it)

                    def silu(c):
                        act.wait_ge(used, before + (MOE0 + (0 if c == 0 else 6 * c - 2) + 2))
                        nc.scalar.activation(sil[c % 2][:, :], pair[c % 2][0][:, :], ACT.Silu).then_inc(m_sil, 1)

                    def a_split(c):
                        act.wait_ge(m_tr, it * CE + (c + 1))
                        if c >= 2:
                            act.wait_ge(used, before + (MOE0 + 6 * (c - 1) + 4))
                        else:
                            act.wait_ge(used, before + MOE0)
                        nc.scalar.activation(a_hi[c % 2][:, :], bank[6 + c % 2][:, :], ACT.Copy).then_inc(m_ahi, 1)

                    hi(AHEAD_E, 4)
                    silu(0)
                    for c in range(1, CE):
                        b = 6 * c - 2
                        hi(b - 2 if c > 1 else 4, b + 4)
                        silu(c)
                        a_split(c - 1)
                    hi(6 * CE - 4, 6 * CE)
                    a_split(CE - 1)
                    gather_hi(it + 1)
                    hi(NE_PIECE, NE_PIECE + AHEAD_E - 1)
                    act.wait_ge(used, before + (MOE0 + NE_PIECE))
                    for b in range(2):
                        nc.scalar.activation(y_hi[:, b * 512:(b + 1) * 512], bank[4 + b][:, :], ACT.Copy,
                                             scale=gslot[:, 0:1]).then_inc(y_hi_done, 1)
                    hi(NE_PIECE + AHEAD_E - 1, NE_PIECE + AHEAD_E)
            norm(7, last_adds=n_pass * (4 * E))

        @block.vector
        def _(dve):
            steps = [0]

            def done(ins):
                steps[0] += 1
                ins.then_inc(chain, 1)
                return steps[0]

            def link(ins):
                dve.wait_ge(chain, done(ins))

            qn = [0]

            def lo_upto(q):
                while qn[0] <= q:
                    split_lo(dve, qn[0], SIZES[qn[0]] if qn[0] < MOE0 else PIECE)
                    qn[0] += 1

            def square(src, c):
                cols = slice(c * 512, (c + 1) * 512)
                return done(nc.vector.tensor_tensor_reduce(out=xn[:, 1, cols], in0=src[:, 1, cols], in1=src[:, 1, cols],
                                                           scale=1.0, scalar=0.0, op0=ALU.mult, op1=ALU.add,
                                                           accum_out=part[:, 1, c:c + 1]))

            def norm(n, src=res, landed=None):
                if landed is not None:
                    dve.wait_ge(landed, 16)
                    for c in range(2):
                        last = square(src, c)
                    dve.wait_ge(chain, last)
                dve.wait_ge(squared, 2 * n + 2)
                nc.vector.tensor_tensor(ss, part[:, :, 0], part[:, :, 1], ALU.add).then_inc(norm_ss, 1)
                dve.wait_ge(norm_sd, n + 1)
                link(nc.vector.reciprocal(rstd, sd))
                if n == 0:
                    dve.wait_ge(s_gain0, 16)
                else:
                    dve.wait_ge(s_gain, 16 * n)
                order = [(t, c) for c in range(2) for t in range(NT)]
                for t, c in (sorted(order) if n == 7 else order):
                    cols = slice(c * 512, (c + 1) * 512)
                    nc.vector.scalar_tensor_tensor(out=xn[:, t, cols], in0=src[:, t, cols], scalar=rstd[:, t:t + 1],
                                                   in1=gain[:, cols], op0=ALU.mult,
                                                   op1=ALU.mult).then_inc(norm_x, 1)

            def norm_split(n):
                for g in range(2):
                    for t in range(NT):
                        i = 2 * g + t
                        dve.wait_ge(norm_hi, 4 * n + i + 1)
                        dst = act_lo[:, 4 * g:4 * g + 4, t * P:(t + 1) * P]
                        nc.vector.tensor_tensor(dst, bank[4 + i][:, :].rearrange("p (k s) -> p k s", k=4),
                                                act_hi[:, 4 * g:4 * g + 4, t * P:(t + 1) * P].bitcast(F32),
                                                ALU.subtract).then_inc(norm_lo, 1)

            def chunk_out(n):
                dve.wait_ge(pair_free[n % 2], n // 2 + 1)

            def add_half(c, banks):
                cols = slice(c * 512, (c + 1) * 512)
                nc.vector.tensor_tensor(res[:, 0, cols], banks[0][:, :], res[:, 0, cols], ALU.add).then_inc(res_added, 1)
                return nc.vector.tensor_tensor(res[:, 1, cols], banks[1][:, :], res[:, 1, cols], ALU.add)

            def add_chunks(q0, n0):
                for c in range(2):
                    n = n0 + c
                    lo_upto(q0 + 2 * c + 1 + AHEAD)
                    dve.wait_ge(used, q0 + 2 * c + 2)
                    add_half(c, pair[n % 2]).then_inc(pair_free[n % 2], 1)
                    dve.wait_ge(pair_free[n % 2], n // 2 + 1)
                    last = square(res, c)
                dve.wait_ge(chain, last)

            nc.vector.memset(eps_col, EPS).then_inc(eps_set, 1)
            dve.wait_ge(s_x[1], 16)
            norm(0, landed=s_x[0])
            lo_upto(0)
            norm_split(0)
            for layer in range(2):
                conf = z[:, 11:14, :]
                q0, n0 = BASE[layer]["win"]
                norm_i = 0
                if layer:
                    norm_i = 4
                    norm(4)
                    norm_split(4)
                lo_upto(q0 + 1 + AHEAD)
                if layer == 0:
                    norm(1, v, s_mem)
                lo_upto(q0 + 3 + AHEAD)
                if layer == 0:
                    dve.wait_ge(par_t, 1)
                    nc.vector.tensor_copy(par[:, 0:NROW], bank[4][:, 0:NROW])
                    nc.vector.tensor_copy(par[:, NROW:NROW + NCW], bank[4][:, P:P + NCW])
                    nc.vector.tensor_copy(par[:, NROW + NCW:], bank[4][:, 2 * P:2 * P + NCW]).then_inc(par_c, 1)
                chunk_out(n0)
                chunk_out(n0 + 1)
                dve.wait_ge(pads, 1)
                dve.wait_ge(par_c, 1)
                ins = nc.vector.tensor_tensor(hpad[:, :, TAPS - 1:], conf, z[:, 14:17, :], ALU.mult)
                ins.then_inc(mix_dve, 1)
                dve.wait_ge(mix_dve, step(MIX_DVE, "prod", layer))

                todo = [(k, b) for k in range(TAPS) for b in range(NCONF) if (b, k) not in conv_taps_pe[layer]]

                def conv_taps():
                    for k, b in todo:
                        acc = z[:, 11 + b, :]
                        src = hpad[:, b, k:k + S]
                        col = NROW + layer * NCW + k * NCONF + b
                        w = par[:, col:col + 1]
                        if k == 0:
                            cb = ROWS["conf_b"] + layer * NCONF + b
                            ins = nc.vector.tensor_scalar(acc, src, w, par[:, cb:cb + 1], ALU.mult, ALU.add)
                        else:
                            dve.wait_ge(chain, conv_at[b])
                            ins = nc.vector.scalar_tensor_tensor(out=acc, in0=src, scalar=w, in1=acc, op0=ALU.mult,
                                                                 op1=ALU.add)
                        if (k, b) == todo[-1] and not CONV_PE[layer]:
                            ins.then_inc(mix_dve, 1)
                        else:
                            conv_at[b] = done(ins)
                        yield

                conv_at = [0] * NCONF
                taps = conv_taps()

                def some_taps(n):
                    for _ in range(n):
                        next(taps, None)

                def pieces_with_taps(first, last, n):
                    for q in range(first, last + 1):
                        lo_upto(q + AHEAD)
                        some_taps(n)

                def a(name):
                    dve.wait_ge(mix_act, step(MIX_ACT, name, layer))

                def short_conv():
                    for n in (n0 + 3, n0 + 4):
                        chunk_out(n)
                    link(nc.vector.tensor_tensor(spad[:, :, SCTAPS - 1:], z[:, 8:11, :], z[:, 2:5, :], ALU.mult))
                    sc_at = [0] * NSC
                    for k in range(SCTAPS):
                        for b in range(NSC):
                            acc = z[:, 2 + b, :]
                            col = ROWS["sconv_w"] + (layer * SCTAPS + k) * NSC + b
                            w = par[:, col:col + 1]
                            if k == 0:
                                ins = nc.vector.tensor_scalar(acc, spad[:, b, k:k + S], w, None, ALU.mult)
                            else:
                                dve.wait_ge(chain, sc_at[b])
                                ins = nc.vector.scalar_tensor_tensor(out=acc, in0=spad[:, b, k:k + S], scalar=w,
                                                                     in1=acc, op0=ALU.mult, op1=ALU.add)
                            sc_at[b] = done(ins)
                    dve.wait_ge(chain, sc_at[-1])
                    nc.vector.tensor_tensor(z[:, 2:5, :], z[:, 2:5, :], z[:, 5:8, :], ALU.mult).then_inc(mix_dve, 1)

                def pool_y():
                    dve.wait_ge(mix_pe, step(MIX_PE, "pool", layer))
                    for b in range(NPOOL):
                        c = ROWS["pool_scale"] + layer * NPOOL + b
                        ins = nc.vector.tensor_scalar(z[:, b, :], bank[6][:, b * S:(b + 1) * S], par[:, c:c + 1],
                                                      None, ALU.mult)
                    ins.then_inc(mix_dve, 1)

                def normalised(sd_name, row, blocks):
                    a(sd_name)
                    link(nc.vector.reciprocal(stat[:, row, :], stat[:, row, :]))
                    for k in blocks:
                        c = ROWS["group_norm_g"] + layer * KD + k
                        ins = nc.vector.scalar_tensor_tensor(out=z[:, k, :], in0=z[:, k, :], scalar=par[:, c:c + 1],
                                                             in1=stat[:, row, :], op0=ALU.mult, op1=ALU.mult)
                    ins.then_inc(mix_dve, 1)

                if layer == 0:
                    pieces_with_taps(q0 + 4, q0 + 7, 8)
                    lo_upto(q0 + 8 + AHEAD)
                    norm_split(1)
                    short_conv()
                    q1, n1 = BASE[0]["kv"]
                    pieces_with_taps(q1, q1 + 3, 6)
                    pool_y()
                    pieces_with_taps(q1 + 4, q1 + 5, 6)
                    normalised("sconv_sd", 4, (2, 3, 4))
                    pieces_with_taps(q1 + 6, q1 + 6, 6)
                    normalised("pool_sd", 3, (0, 1))
                else:
                    pieces_with_taps(q0 + 4, q0 + 7, 7)
                    pool_y()
                    pieces_with_taps(q0 + 8, q0 + 8, 3)
                    short_conv()
                    normalised("pool_sd", 3, (0, 1))
                    some_taps(3)
                    normalised("sconv_sd", 4, (2, 3, 4))
                q0, n0 = BASE[layer]["wout"]
                for name, b0, b1 in (("pool", 0, 2), ("sconv", 2, 5)):
                    a("hi_" + name)
                    nc.vector.tensor_tensor(act_lo[:, b0:b1, :], z[:, b0:b1, :],
                                            act_hi[:, b0:b1, :].bitcast(F32), ALU.subtract).then_inc(mix_dve, 1)
                lo_upto(q0 + 2)
                some_taps(TAPS * NCONF)
                if CONV_PE[layer]:
                    dve.wait_ge(conv_act, 1)
                    dve.wait_ge(chain, max(conv_at))
                    nc.vector.tensor_tensor(z[:, 11 + CONV_PART, :], bank[7][:, S:2 * S], z[:, 11 + CONV_PART, :],
                                            ALU.add).then_inc(mix_dve, 1)
                lo_upto(q0 + 3)
                dve.wait_ge(mix_pe, step(MIX_PE, "mean", layer))
                nc.vector.tensor_tensor(conf, conf, bank[6][:, 0:S].rearrange("p (a s) -> p a s", a=1).broadcast_to(
                    [P, NCONF, S]), ALU.subtract).then_inc(mix_dve, 1)
                for c in range(2):
                    n = n0 + c
                    cols = slice(c * 512, (c + 1) * 512)
                    dve.wait_ge(group_a, 2 * layer + c + 1)
                    for t in range(NT):
                        ins = nc.vector.tensor_tensor(res[:, t, cols], pair[n % 2][t][:, :], res[:, t, cols], ALU.add)
                    ins.then_inc(pair_free[n % 2], 1)
                a("conf_sd")
                link(nc.vector.reciprocal(stat[:, 2, :], stat[:, 1, :]))
                for b in range(NCONF):
                    nc.vector.tensor_tensor(z[:, 11 + b, :], z[:, 11 + b, :], stat[:, 2, :],
                                            ALU.mult).then_inc(mix_dve, 1)
                for b in range(NCONF):
                    c = ROWS["group_norm_g"] + layer * KD + 5 + b
                    a(f"hi_conf{b}")
                    nc.vector.scalar_tensor_tensor(out=act_lo[:, 5 + b, :], in0=z[:, 11 + b, :], scalar=par[:, c:c + 1],
                                                   in1=act_hi[:, 5 + b, :].bitcast(F32), op0=ALU.mult,
                                                   op1=ALU.subtract).then_inc(mix_dve, 1)
                lo_upto(q0 + N_SQ - 1 + AHEAD)
                a("rms_sd")
                link(nc.vector.reciprocal(group_rstd, group_sd))
                for c in range(2):
                    n = n0 + 2 + c
                    if c == 0:
                        dve.wait_ge(out_half, layer + 1)
                    else:
                        dve.wait_ge(used, q0 + N_SQ)
                    cols = slice(c * 512, (c + 1) * 512)
                    for t in range(NT):
                        nc.vector.scalar_tensor_tensor(out=res[:, t, cols], in0=pair[n % 2][t][:, :],
                                                       scalar=group_rstd[:, t:t + 1], in1=res[:, t, cols], op0=ALU.mult,
                                                       op1=ALU.add).then_inc(pair_free[n % 2] if t else res_added, 1)
                    dve.wait_ge(pair_free[n % 2], n // 2 + 1)
                    last = square(res, c)
                dve.wait_ge(chain, last)
                norm_i += 2 if layer == 0 else 1
                norm(norm_i)
                norm_split(norm_i)
                lo_upto(BASE[layer]["wq"][0] + N_SQ - 1 + AHEAD)
                for h in range(HEADS):
                    dve.wait_ge(scores, layer * HEADS + h + 1)
                    link(nc.vector.tensor_reduce(top_sum[:, 2 * h:2 * h + 2],
                                                 bank[4 + h][:, :].rearrange("p (t s) -> p t s", t=NT), AX.X, ALU.max))
                    nc.vector.tensor_scalar(top_neg[:, 2 * h:2 * h + 2], top_sum[:, 2 * h:2 * h + 2], -1.0 / 16, None,
                                            ALU.mult).then_inc(top, 1)
                for h in range(HEADS):
                    dve.wait_ge(probs, layer * HEADS + h + 1)
                    link(nc.vector.reciprocal(top_inv[:, 2 * h:2 * h + 2], top_sum[:, 2 * h:2 * h + 2]))
                    for t in range(NT):
                        i = 2 * h + t
                        ins = nc.vector.tensor_scalar(z[:, i, :], z[:, i, :], top_inv[:, i:i + 1], None, ALU.mult)
                    ins.then_inc(normed, 1)
                for h in range(1, HEADS, 2):
                    dve.wait_ge(pt, layer * HEADS + h + 1)
                    nc.vector.tensor_copy(z[:, 8 + 2 * h:10 + 2 * h, :],
                                          bank[4 + h][:, :].rearrange("p (b s) -> p b s", s=S)).then_inc(pt_odd, 1)
                for h in range(HEADS):
                    dve.wait_ge(o_hi, layer * HEADS + h + 1)
                    nc.vector.tensor_tensor(act_lo[:, 2 * h:2 * h + 2, :],
                                            bank[4 + h][:, :].rearrange("p (b s) -> p b s", s=S),
                                            act_hi[:, 2 * h:2 * h + 2, :].bitcast(F32), ALU.subtract).then_inc(o_lo, 1)
                add_chunks(*BASE[layer]["wo"])
                norm_i += 1
                norm(norm_i)
                norm_split(norm_i)
                if layer == 0:
                    q0, n0 = BASE[0]["ffn"]
                    for j in range(NF):
                        lo_upto(q0 + ffn_piece("up", j) + AHEAD)
                        dve.wait_ge(used, q0 + ffn_piece("up", j) + 1)
                        dve.wait_ge(f_silu, j + 1)
                        if j >= 2:
                            dve.wait_ge(f_ahi, j - 1)
                        ins = nc.vector.tensor_tensor(f_a[j % 2][:, :], pair[j % 2][1][:, :], f_sil[j % 2][:, :], ALU.mult)
                        ins.then_inc(f_prod, 1)
                        dve.wait_ge(f_ahi, j + 1)
                        nc.vector.tensor_tensor(f_lo[j % 2][:, :], f_a[j % 2][:, :], f_hi[j % 2][:, :].bitcast(F32),
                                                ALU.subtract).then_inc(f_alo, 1)
                    lo_upto(q0 + N_FFN - 1 + AHEAD)
                    for c in range(2):
                        if c == 0:
                            dve.wait_ge(ffn_half, 1)
                        else:
                            dve.wait_ge(used, q0 + N_FFN)
                        link(add_half(c, (bank[4 + c], bank[6 + c])))
                        last = square(res, c)
                    dve.wait_ge(chain, last)
            dve.wait_ge(wr_split, 1)
            nc.vector.tensor_tensor(wr_lo[:, :, :], wr[:, :, :], wr_hi[:, :, :].bitcast(F32),
                                    ALU.subtract).then_inc(wr_split, 1)
            lo_upto(MOE0 + AHEAD_E - 1)
            dve.wait_ge(logits_t, 1)
            nc.vector.tensor_copy(logit[:, :], bank[4][0:E, 0:S]).then_inc(logits_copied, 1)
            dve.wait_ge(logits, 1)
            for t in range(NT):
                last = done(nc.vector.max(best[:, t, :], bank[5][:, t * E:(t + 1) * E]))
            dve.wait_ge(chain, last)
            for t in range(NT):
                last = done(nc.vector.max_index(idx8[:, t, :], best[:, t, :], bank[5][:, t * E:(t + 1) * E]))
            nc.vector.tensor_tensor(diff[:, :, :], best[:, :, 1:2], best[:, :, 0:1],
                                    ALU.subtract).then_inc(margins, 1)
            dve.wait_ge(chain, last)
            link(nc.vector.tensor_copy(idx[:, :, :], idx8[:, :, :]))
            iota8 = cst[:, C_IOTA8:C_IOTA8 + E].rearrange("p (a e) -> p a e", a=1).broadcast_to([P, NT, E])
            for j in range(2):
                last = done(nc.vector.tensor_tensor(hot[:, j, :, :], idx[:, :, j:j + 1].broadcast_to([P, NT, E]), iota8,
                                                    ALU.is_equal))
            dve.wait_ge(chain, last)
            nc.vector.tensor_tensor(mask[:, :, :], hot[:, 0, :, :], hot[:, 1, :, :], ALU.add).then_inc(masks, 1)
            dve.wait_ge(tok_split, 1)
            nc.vector.tensor_tensor(tok_lo[:, :, :], xn[:, :, :], tok_hi[:, :, :].bitcast(F32),
                                    ALU.subtract).then_inc(tok_split, 1)
            dve.wait_ge(ranks, 1)
            link(nc.vector.scalar_tensor_tensor(out=slot1[:, :, :],
                                                in0=bank[6][:, 0:NT * E].rearrange("p (t e) -> p t e", t=NT),
                                                scalar=1.0, in1=mask[:, :, :], op0=ALU.add, op1=ALU.mult))
            nc.vector.tensor_scalar(rank[:, :, E:2 * E], slot1[:, :, :], float(SLOTS + 1), None, ALU.subtract)
            nc.vector.memset(rank[:, :, 2 * E:], -1.0)
            link(nc.vector.tensor_scalar(rank[:, :, 0:E], slot1[:, :, :], -1.0, None, ALU.add))
            iota = cst[:, C_IOTA:C_IOTA + SLOTS]
            link(nc.vector.tensor_copy(rcol[:, :, :], rank[:, :, 0:1]))
            for t in range(NT):
                ins = nc.vector.tensor_scalar(pick[:, t, :], iota, rcol[:, t, :], None, ALU.is_equal)
            ins.then_inc(picked, 1)
            link(nc.vector.tensor_reduce(cnt[:, 0:1], bank[6][:, NT * E:(NT + 1) * E], AX.X, ALU.max))
            link(nc.vector.tensor_scalar(cnt[:, 1:2], cnt[:, 0:1], float(SLOTS), 1.0, ALU.is_gt, ALU.add))
            nc.vector.tensor_copy(passes[:, :], cnt[:, 1:2]).then_inc(routed, 1)
            link(nc.vector.memset(zero[:, :], 0.0))
            for b in range(2):
                nc.vector.tensor_copy(y_hi[:, b * 512:(b + 1) * 512], zero[:, 0:512])
                nc.vector.tensor_copy(y_lo[:, b * 512:(b + 1) * 512], zero[:, 0:512]).then_inc(y_lo_done, 1)
            nc.vector.tensor_copy(place[:, :], zero[:, 0:S]).then_inc(placed, 1)
            dve.wait_ge(r_exp, 1)
            link(nc.vector.tensor_scalar(gw[:, 1, :, :], ex[:, :, :], 1.0, None, ALU.add))
            link(nc.vector.reciprocal(gw[:, 0, :, :], gw[:, 1, :, :]))
            link(nc.vector.tensor_tensor(gw[:, 1, :, :], ex[:, :, :], gw[:, 0, :, :], ALU.mult))
            for j in range(2):
                last = done(nc.vector.tensor_tensor(hot[:, j, :, :], hot[:, j, :, :],
                                                    gw[:, j, :, :].broadcast_to([P, NT, E]), ALU.mult))
            dve.wait_ge(chain, last)
            for half in range(2):
                nc.vector.tensor_tensor(gate[:, :, half * E:(half + 1) * E], hot[:, 0, :, :], hot[:, 1, :, :], ALU.add)
            nc.vector.memset(gate[:, :, 2 * E:], 0.0)

            def gather_lo(r):
                for b in range(2):
                    dve.wait_ge(xe_hi_done, r * 2 + (b + 1))
                    nc.vector.tensor_tensor(xe_lo[:, 4 * b:4 * b + 4, :],
                                            pair[1][b][:, :].rearrange("p (k s) -> p k s", k=4),
                                            xe_hi[:, 4 * b:4 * b + 4, :].bitcast(F32), ALU.subtract).then_inc(xe_lo_done, 1)

            gather_lo(0)

            def add_combined(r, t, banks=bank[6:8]):
                for b in range(2):
                    dve.wait_ge(combined, r * 4 + (2 * t + b + 1))
                    cols = res[:, t, b * 512:(b + 1) * 512]
                    nc.vector.tensor_tensor(cols, banks[b][:, :], cols, ALU.add).then_inc(added, 1)

            dve.wait_ge(routed, 1)
            n_pass = dve.value_load(passes[0:1, 0:1], min_val=1, max_val=2)
            own = 2
            with dve.Fori(0, n_pass) as ps:
                with dve.Fori(0, E) as e:
                    it = ps * E + e
                    before = it * NE_PIECE

                    def lo(i0, i1):
                        for i in range(i0, i1):
                            split_lo(dve, MOE0 + i, it=it)

                    def product(c):
                        dve.wait_ge(used, before + (MOE0 + (0 if c == 0 else 6 * c - 2) + 4))
                        dve.wait_ge(m_sil, it * CE + (c + 1))
                        nc.vector.tensor_tensor(prod[c % 2][:, :], pair[c % 2][1][:, :], sil[c % 2][:, :],
                                                ALU.mult).then_inc(m_prod, 1)

                    def a_split(c):
                        dve.wait_ge(m_ahi, it * CE + (c + 1))
                        nc.vector.tensor_tensor(a_lo[c % 2][:, :], bank[6 + c % 2][:, :], a_hi[c % 2][:, :].bitcast(F32),
                                                ALU.subtract).then_inc(m_alo, 1)

                    def own_wait(k):
                        dve.wait_ge(loop_chain, it * own + k)

                    lo(AHEAD_E, 4)
                    add_combined(it, 0)
                    lo(4, 6)
                    add_combined(it, 1)
                    product(0)
                    nc.vector.tensor_copy(gcol[:, :, :], gate[:, :, bass.ds(it, 1)]).then_inc(loop_chain, 1)
                    nc.vector.tensor_copy(rcol[:, :, :], rank[:, :, bass.ds(it + 1, 1)]).then_inc(loop_chain, 1)
                    own_wait(2)
                    for t in range(NT):
                        ins = nc.vector.tensor_scalar(gpick[:, t, :], pick[:, t, :].bitcast(F32), gcol[:, t, :], None,
                                                      ALU.mult)
                    ins.then_inc(gpicked, 1)
                    dve.wait_ge(gpicked, it + 1)
                    for t in range(NT):
                        ins = nc.vector.tensor_scalar(pick[:, t, :], iota, rcol[:, t, :], None, ALU.is_equal)
                    ins.then_inc(picked, 1)
                    lo(6, 8)
                    a_split(0)
                    lo(8, 10)
                    product(1)
                    lo(10, 12)
                    dve.wait_ge(placed_t, it + 1)
                    nc.vector.tensor_reduce(gslot[:, :], bank[7][:, 0:S], AX.X, ALU.add)
                    nc.vector.tensor_scalar(place[:, :], bank[7][:, 0:S], 0.0, None, ALU.is_gt).then_inc(placed, 1)
                    for c in range(2, CE):
                        b = 6 * c - 2
                        lo(b + 2, b + 4)
                        a_split(c - 1)
                        lo(b + 4, b + 6)
                        product(c)
                        if c < CE - 1:
                            lo(b + 6, b + 8)
                    lo(6 * CE - 2, 6 * CE)
                    a_split(CE - 1)
                    gather_lo(it + 1)
                    lo(NE_PIECE, NE_PIECE + AHEAD_E - 1)
                    for b in range(2):
                        dve.wait_ge(y_hi_done, it * 2 + (b + 1))
                        cols = slice(b * 512, (b + 1) * 512)
                        nc.vector.scalar_tensor_tensor(out=y_lo[:, cols], in0=bank[4 + b][:, :], scalar=gslot[:, 0:1],
                                                       in1=y_hi[:, cols].bitcast(F32), op0=ALU.mult,
                                                       op1=ALU.subtract).then_inc(y_lo_done, 1)
                    lo(NE_PIECE + AHEAD_E - 1, NE_PIECE + AHEAD_E)
            rounds = n_pass * E
            add_combined(rounds, 0)
            add_combined(rounds, 1, pair[0])
            for c in range(2):
                dve.wait_ge(added, rounds * 4 + (3 + c))
                last = square(res, c)
            dve.wait_ge(chain, last)
            norm(7)

        @block.tensor
        def _(pe):
            mm = nc.tensor.matmul

            def norm_transpose(n):
                for g in range(2):
                    for t in range(NT):
                        pe.wait_ge(norm_x, 4 * n + 2 * g + t + 1)
                        for k in range(4):
                            kk = 4 * g + k
                            ins = nc.tensor.transpose(bank[4 + 2 * g + t][:, k * P:(k + 1) * P],
                                                      xn[:, t, kk * P:(kk + 1) * P], ident)
                        ins.then_inc(norm_t, 1)

            def take(q, nk, it=None):
                pe.wait_ge(lo_done, q + 1 if it is None else it * NE_PIECE + (q + 1))
                n = (SIZES[q] if q < MOE0 else PIECE) // nk
                return [w[q % SPLIT][:, 0:nk * n].rearrange("p (k n) -> p k n", k=nk) for w in (w_hi, w_lo)]

            def columns(q, banks, k0, nk, nb, first, last):
                hi, lo = take(q, nk)
                for b in range(nb):
                    dst = banks[b // 2][:, (b % 2) * S:(b % 2) * S + S]
                    cols = slice(b * P, (b + 1) * P)
                    for k in range(nk):
                        begin = first and k == 0 and b % 2 == 0
                        end = last and k == nk - 1
                        mm(dst, hi[:, k, cols], act_hi[:, k0 + k, :], start=begin, stop=False, skip_group_check=True)
                        mm(dst, hi[:, k, cols], act_lo[:, k0 + k, :], start=False, stop=False, skip_group_check=True)
                        ins = mm(dst, lo[:, k, cols], act_hi[:, k0 + k, :], start=False, stop=end,
                                 skip_group_check=True)
                ins.then_inc(used, 1)

            def tokens(q, banks, k0, first, last):
                hi, lo = take(q, 4)
                for t in range(NT):
                    for k in range(4):
                        ah, al = (x_[:, k0 + k, t * P:(t + 1) * P] for x_ in (act_hi, act_lo))
                        mm(banks[t][:, :], ah, hi[:, k, :], start=first and k == 0, stop=False)
                        mm(banks[t][:, :], ah, lo[:, k, :], start=False, stop=False)
                        ins = mm(banks[t][:, :], al, hi[:, k, :], start=False, stop=last and k == 3)
                ins.then_inc(used, 1)

            def free_pair(n):
                if n >= 2:
                    pe.wait_ge(pair_free[n % 2], n // 2)

            def product(q0, n0, chunks, how, norm_i=None):
                for c in range(chunks):
                    n = n0 + c
                    free_pair(n)
                    for half in range(2):
                        q = q0 + 2 * c + half
                        if norm_i is not None and c == 0:
                            pe.wait_ge(norm_lo, 4 * norm_i + 2 * half + 2)
                        if how == "columns":
                            columns(q, pair[n % 2], 4 * half, 4, 4, half == 0, half == 1)
                        else:
                            tokens(q, pair[n % 2], 4 * half, half == 0, half == 1)

            pe.wait_ge(s_cst, 16)
            norm_transpose(0)
            for layer in range(2):
                norm_i = 0 if layer == 0 else 4
                if layer:
                    norm_transpose(4)
                def col_sum(dst, src, blocks, by=ones):
                    for i, b in enumerate(blocks):
                        ins = mm(dst, by, src[:, b, :], start=i == 0, stop=i == len(blocks) - 1)
                    ins.then_inc(mix_pe, 1)

                def pool_product():
                    pe.wait_ge(mix_pool, layer + 1)
                    pe.wait_ge(s_pw, 16 * 8)
                    for b in range(NPOOL):
                        ins = mm(bank[6][:, b * S:(b + 1) * S], pool_bd[:, layer * NPOOL + b, :], z[:, b, :],
                                 start=True, stop=True)
                    ins.then_inc(mix_pe, 1)

                def sconv_sum():
                    pe.wait_ge(mix_act, step(MIX_ACT, "sconv_sq", layer))
                    col_sum(bank[4][:, 0:S], z_sq, (2, 3, 4))

                def pool_sum():
                    pe.wait_ge(mix_act, step(MIX_ACT, "pool_sq", layer))
                    col_sum(bank[5][:, 0:S], z_sq, (0, 1))

                q0, n0 = BASE[layer]["win"]
                product(q0, n0, 1, "columns", norm_i)
                product(q0 + 2, n0 + 1, 1, "columns")
                if layer == 0:
                    pe.wait_ge(s_rows, 16 * 8)
                    nc.tensor.transpose(bank[4][:, 0:NROW], rows[0:NROW, 0, :], ident[0:NROW, 0:NROW])
                    nc.tensor.transpose(bank[4][:, P:P + NCW], rows[0:NCW, 1, :], ident[0:NCW, 0:NCW])
                    nc.tensor.transpose(bank[4][:, 2 * P:2 * P + NCW], rows[0:NCW, 2, :],
                                        ident[0:NCW, 0:NCW]).then_inc(par_t, 1)
                product(q0 + 4, n0 + 2, 2, "columns")
                if layer:
                    pool_product()
                else:
                    pe.wait_ge(par_c, 1)
                    norm_transpose(1)
                free_pair(n0 + 4)
                columns(q0 + 8, pair[(n0 + 4) % 2], 0, KD, 1, True, True)
                if layer == 0:
                    q1, n1 = BASE[0]["kv"]
                    product(q1, n1, 1, "columns", 1)
                    pool_product()
                    product(q1 + 2, n1 + 1, 1, "columns")
                    sconv_sum()
                    product(q1 + 4, n1 + 2, 1, "tokens")
                    pool_sum()
                    product(q1 + 6, n1 + 3, 1, "tokens")
                else:
                    for i, (b, k) in enumerate(conv_taps_pe[layer]):
                        first = (b, k) in CONV_PE[layer]
                        dst = bank[7][:, 0:S] if b == CONV_FULL else bank[7][:, S:2 * S]
                        pe.wait_ge(diags, i + 1)
                        ins = mm(dst, diag[i], hpad[:, b, k:k + S], start=first, stop=k == TAPS - 1)
                        if i == 6:
                            pool_sum()
                        elif i == 25:
                            sconv_sum()
                    ins.then_inc(conv_pe, 1)

                q0, n0 = BASE[layer]["wout"]

                def out_rows(q, at, blocks, n, first=False, last=False):
                    hi, lo = take(q, 2)
                    for c in range(2):
                        if first:
                            free_pair(n + c)
                        w = slice(c * 512, (c + 1) * 512)
                        for t in range(NT):
                            dst = pair[(n + c) % 2][t][:, :]
                            for i, k in enumerate(blocks):
                                ah, al = (x_[:, k, t * P:(t + 1) * P] for x_ in (act_hi, act_lo))
                                mm(dst, ah, hi[:, at + i, w], start=first and i == 0, stop=False)
                                mm(dst, ah, lo[:, at + i, w], start=False, stop=False)
                                ins = mm(dst, al, hi[:, at + i, w], start=False, stop=last and i == len(blocks) - 1)
                        if k == 4:
                            ins.then_inc(group_a, 1)
                        elif c == 0 and k == KD - 1:
                            ins.then_inc(out_half, 1)
                    return ins

                pe.wait_ge(mix_dve, step(MIX_DVE, "lo_pool", layer))
                out_rows(q0, 0, (0, 1), n0, first=True).then_inc(used, 1)
                pe.wait_ge(mix_dve, step(MIX_DVE, "lo_sconv", layer))
                out_rows(q0 + 1, 0, (2, 3), n0).then_inc(used, 1)
                pe.wait_ge(mix_dve, step(MIX_DVE, "conv", layer))
                if CONV_PE[layer]:
                    pe.wait_ge(conv_act, 1)
                col_sum(bank[6][:, 0:S], z, (11, 12, 13), cst[:, C_MEAN:C_MEAN + P])
                out_rows(q0 + 2, 0, (4,), n0, last=True)
                pe.wait_ge(mix_act, step(MIX_ACT, "conf_sq", layer))
                col_sum(bank[5][:, 0:S], z_sq, (5, 6, 7))
                pe.wait_ge(mix_dve, step(MIX_DVE, "lo_conf0", layer))
                out_rows(q0 + 2, 1, (5,), n0 + 2, first=True).then_inc(used, 1)
                pe.wait_ge(mix_act, step(MIX_ACT, "rms_sq", layer))
                for t in range(NT):
                    for b in (5, 6, 7):
                        ins = mm(bank[4][:, t:t + 1], z_sq[:, b, t * P:(t + 1) * P], ones[:, 0:1], start=b == 5,
                                 stop=b == 7)
                ins.then_inc(mix_pe, 1)
                pe.wait_ge(mix_dve, step(MIX_DVE, "lo_conf2", layer))
                out_rows(q0 + 3, 0, (6, 7), n0 + 2, last=True).then_inc(used, 1)
                norm_i += 2 if layer == 0 else 1
                norm_transpose(norm_i)
                q0, n0 = BASE[layer]["wq"]
                product(q0, n0, 2, "columns", norm_i)
                for n in (n0, n0 + 1):
                    pe.wait_ge(pair_free[n % 2], n // 2 + 1)
                for h in range(HEADS):
                    for t in range(NT):
                        for b in range(2):
                            k = 2 * h + b
                            ins = mm(bank[4 + h][:, t * S:(t + 1) * S], scr[:, k, t * P:(t + 1) * P], kT[:, k, :],
                                     start=b == 0, stop=b == 1)
                    ins.then_inc(scores, 1)
                for h in range(HEADS):
                    pe.wait_ge(normed, layer * HEADS + h + 1)
                    for mb in range(NT):
                        for t in range(NT):
                            ins = nc.tensor.transpose(bank[4 + h][:, mb * S + t * P:mb * S + (t + 1) * P],
                                                      z[:, 2 * h + t, mb * P:(mb + 1) * P], ident)
                    ins.then_inc(pt, 1)
                for h in range(HEADS):
                    pe.wait_ge(pt_odd if h % 2 else pt_even, layer * 2 + h // 2 + 1)
                    for b in range(2):
                        for mb in range(NT):
                            ins = mm(bank[4 + h][:, b * S:(b + 1) * S], v[:, mb, (2 * h + b) * P:(2 * h + b + 1) * P],
                                     z[:, 8 + 2 * h + mb, :], start=mb == 0, stop=mb == NT - 1)
                    ins.then_inc(attn_o, 1)
                pe.wait_ge(o_lo, (layer + 1) * HEADS)
                product(*BASE[layer]["wo"], 2, "tokens")
                norm_i += 1
                norm_transpose(norm_i)
                pe.wait_ge(norm_lo, 4 * (norm_i + 1))
                if layer == 0:
                    q0, n0 = BASE[0]["ffn"]

                    def down(j):
                        hi, lo = take(q0 + ffn_piece("down", j), 2)
                        pe.wait_ge(f_alo, j + 1)
                        for c in range(2):
                            w = slice(c * 512, (c + 1) * 512)
                            for t in range(NT):
                                dst = bank[4 + 2 * t + c][:, :]
                                for b in range(2):
                                    cols = slice(b * S + t * P, b * S + (t + 1) * P)
                                    ah, al = f_hi[j % 2][:, cols], f_lo[j % 2][:, cols]
                                    begin, end = j == 0 and b == 0, j == NF - 1 and b == 1
                                    mm(dst, ah, hi[:, b, w], start=begin, stop=False)
                                    mm(dst, ah, lo[:, b, w], start=False, stop=False)
                                    ins = mm(dst, al, hi[:, b, w], start=False, stop=end)
                            if c == 0 and j == NF - 1:
                                ins.then_inc(ffn_half, 1)
                        ins.then_inc(used, 1)

                    for j in range(NF):
                        if j >= 2:
                            pe.wait_ge(f_prod, j - 1)
                        columns(q0 + ffn_piece("gate", j), (pair[j % 2][0],), 0, KD, 2, True, True)
                        columns(q0 + ffn_piece("up", j), (pair[j % 2][1],), 0, KD, 2, True, True)
                        if j:
                            down(j - 1)
                    down(NF - 1)
            pe.wait_ge(wr_split, 2)
            for k in range(KD):
                dst = bank[4][0:E, 0:S]
                mm(dst, wr_hi[:, k, :], act_hi[:, k, :], start=k == 0, stop=False)
                mm(dst, wr_lo[:, k, :], act_hi[:, k, :], start=False, stop=False)
                ins = mm(dst, wr_hi[:, k, :], act_lo[:, k, :], start=False, stop=k == KD - 1)
            ins.then_inc(logits_t, 1)
            pe.wait_ge(logits_copied, 1)
            for t in range(NT):
                ins = nc.tensor.transpose(bank[5][:, t * E:(t + 1) * E], logit[:, t * P:(t + 1) * P], ident[0:E, 0:E])
            ins.then_inc(logits, 1)
            pe.wait_ge(masks, 1)
            tri = cst[:, C_TRI:C_TRI + P]
            mm(bank[6][:, 0:E], tri, mask[:, 0, :], start=True, stop=True)
            mm(bank[6][:, E:2 * E], ones, mask[:, 0, :], start=True, stop=False)
            mm(bank[6][:, E:2 * E], tri, mask[:, 1, :], start=False, stop=True)
            mm(bank[6][:, 2 * E:3 * E], ones, mask[:, 0, :], start=True, stop=False)
            mm(bank[6][:, 2 * E:3 * E], ones, mask[:, 1, :], start=False, stop=True).then_inc(ranks, 1)

            def gather(r):
                pe.wait_ge(picked, r + 1)
                for k in range(KD):
                    dst = pair[1][k // 4][:, (k % 4) * SLOTS:(k % 4 + 1) * SLOTS]
                    for t in range(NT):
                        cols = slice(k * P, (k + 1) * P)
                        mm(dst, tok_hi[:, t, cols], pick[:, t, :], start=t == 0, stop=False)
                        ins = mm(dst, tok_lo[:, t, cols], pick[:, t, :], start=False, stop=t == NT - 1)
                    if k % 4 == 3:
                        ins.then_inc(gathered, 1)

            def combine(r, t, banks=bank[6:8]):
                cols = slice(t * P, (t + 1) * P)
                for b in range(2):
                    w = slice(b * 512, (b + 1) * 512)
                    mm(banks[b][:, :], place[:, cols], y_hi[:, w], start=True, stop=False)
                    mm(banks[b][:, :], place[:, cols], y_lo[:, w], start=False, stop=True).then_inc(combined, 1)

            pe.wait_ge(tok_split, 2)
            gather(0)
            pe.wait_ge(routed, 1)
            n_pass = pe.value_load(passes[0:1, 0:1], min_val=1, max_val=2)
            with pe.Fori(0, n_pass) as ps:
                with pe.Fori(0, E) as e:
                    it = ps * E + e
                    before = it * NE_PIECE

                    def gate_up(c, kind):
                        i0 = (0 if c == 0 else 6 * c - 2) + 2 * kind
                        dst = pair[c % 2][kind][:, :]
                        for half in range(2):
                            if (c, kind) == (0, 0):
                                pe.wait_ge(xe_lo_done, it * 2 + (half + 1))
                            hi, lo = take(MOE0 + i0 + half, 4, it)
                            for k in range(4):
                                kk = 4 * half + k
                                mm(dst, xe_hi[:, kk, :], hi[:, k, :], start=kk == 0, stop=False)
                                mm(dst, xe_hi[:, kk, :], lo[:, k, :], start=False, stop=False)
                                ins = mm(dst, xe_lo[:, kk, :], hi[:, k, :], start=False, stop=kk == KD - 1)
                            ins.then_inc(used, 1)

                    def turn(c):
                        pe.wait_ge(m_prod, it * CE + (c + 1))
                        if c >= 2:
                            pe.wait_ge(m_alo, it * CE + (c - 1))
                        for b in range(4):
                            ins = nc.tensor.transpose(bank[6 + c % 2][:, b * P:(b + 1) * P],
                                                      prod[c % 2][:, b * P:(b + 1) * P], ident)
                        ins.then_inc(m_tr, 1)

                    def down(c):
                        pe.wait_ge(m_alo, it * CE + (c + 1))
                        for half in range(2):
                            hi, lo = take(MOE0 + (6 * c + 8 if c < CE - 1 else 6 * CE - 2) + half, 2, it)
                            for k in range(2):
                                b = 2 * half + k
                                ah, al = (x_[c % 2][:, b * P:(b + 1) * P] for x_ in (a_hi, a_lo))
                                for o in range(2):
                                    w = slice(o * 512, (o + 1) * 512)
                                    begin, end = c == 0 and b == 0, c == CE - 1 and b == 3
                                    mm(bank[4 + o][:, :], ah, hi[:, k, w], start=begin, stop=False)
                                    mm(bank[4 + o][:, :], ah, lo[:, k, w], start=False, stop=False)
                                    ins = mm(bank[4 + o][:, :], al, hi[:, k, w], start=False, stop=end)
                            ins.then_inc(used, 1)

                    gate_up(0, 0)
                    pe.wait_ge(y_lo_done, it * 2 + 2)
                    pe.wait_ge(placed, it + 1)
                    combine(it, 0)
                    gate_up(0, 1)
                    pe.wait_ge(added, it * 4 + 2)
                    combine(it, 1)
                    gate_up(1, 0)
                    pe.wait_ge(added, it * 4 + 4)
                    turn(0)
                    gate_up(1, 1)
                    down(0)
                    pe.wait_ge(gpicked, it + 1)
                    for t in range(NT):
                        ins = nc.tensor.transpose(bank[7][:, t * P:(t + 1) * P], gpick[:, t, :], ident)
                    ins.then_inc(placed_t, 1)
                    for c in range(2, CE):
                        pe.wait_ge(m_prod, it * CE + (c - 1))
                        gate_up(c, 0)
                        if c == 2:
                            pe.wait_ge(placed, it + 2)
                        turn(c - 1)
                        gate_up(c, 1)
                        down(c - 1)
                    turn(CE - 1)
                    gather(it + 1)
                    down(CE - 1)
            rounds = n_pass * E
            pe.wait_ge(y_lo_done, rounds * 2 + 2)
            pe.wait_ge(placed, rounds + 1)
            combine(rounds, 0)
            combine(rounds, 1, pair[0])


_INS = ['x', 'mem', 'mix_norm_g', 'w_in', 'pool_w', 'pool_scale', 'sconv_w', 'conf_w', 'conf_b', 'conf_ln_g',
        'conf_ln_b', 'group_norm_g', 'w_out', 'mem_norm_g', 'w_mem_kv', 'xattn_norm_g', 'w_q', 'w_o', 'ffn_norm_g',
        'w_gu_dense', 'w_down_dense', 'w_router', 'w_gu_moe', 'w_down_moe', 'final_norm_g']
_OUTS = [((1, S, D), 'float32')]


def constants(np):
    t = np.zeros((P, C_ALL), np.float32)
    p = np.arange(P)
    t[:, C_ID:C_ID + P] = np.eye(P)
    t[:, C_ONE:C_ONE + P] = 1.0
    t[:, C_TRI:C_TRI + P] = p[:, None] < p[None, :]
    t[:, C_IOTA:C_IOTA + P] = p[None, :]
    t[:, C_IOTA8:C_IOTA8 + E] = np.arange(E)
    t[:, C_MEAN:C_MEAN + P] = 1.0 / (NCONF * P)
    for b in range(NPOOL):
        for h in range(2):
            count = np.minimum(np.arange(S) + 1, WINDOWS[2 * b + h])
            t[h * P // 2:(h + 1) * P // 2, C_INV + b * S:C_INV + (b + 1) * S] = 1.0 / count
    return t


def kernel(**inputs):
    import numpy as _np
    import concourse.bacc as _bacc
    from concourse import mybir as _mybir
    from concourse.bass_utils import run_bass_kernel_spmd as _run

    nc = _bacc.Bacc("TRN2", target_bir_lowering=False, num_devices=1)
    arrays, args = {}, []
    for name in _INS + ["table"]:
        a = constants(_np) if name == "table" else _np.ascontiguousarray(inputs[name])
        arrays[f"in_{name}_dram"] = a
        args.append(nc.dram_tensor(f"in_{name}_dram", a.shape, _mybir.dt.from_np(a.dtype), kind="ExternalInput").ap())
    for i, (shape, dtype) in enumerate(_OUTS):
        dt = _mybir.dt.from_np(_np.dtype(dtype))
        args.append(nc.dram_tensor(f"out_{i}_dram", shape, dt, kind="ExternalOutput").ap())
    trunk(nc, *args)
    r = _run(nc, [arrays], core_ids=[0])
    got = tuple(r.results[0][f"out_{i}_dram"] for i in range(len(_OUTS)))
    return got[0]
```
